# Optimizing a Trainium2 kernel written in Bass

```python
import jax, jax.numpy as jnp
from jax import lax
import numpy as np
import math

D_MODEL = 1024
BATCH = 1
SEQ = 256
DEPTH = 1

MOBA_HEADS = 8
HEAD_DIM = 64
MOBA_WIDTH = MOBA_HEADS * HEAD_DIM
MOBA_BLOCK = 256
MOBA_TOPK = 3
MOBA_Q_CHUNK = 32
ROPE_THETA = 500000.0
ROPE_DIM = HEAD_DIM // 4
RWKV_HEADS = 8
RWKV_WIDTH = RWKV_HEADS * HEAD_DIM
RWKV_DECAY_LORA = 64
RWKV_AAA_LORA = 64
RWKV_GATE_LORA = 128
RWKV_SHIFT_WIDTH = 3 * RWKV_WIDTH + RWKV_DECAY_LORA + RWKV_AAA_LORA + RWKV_GATE_LORA
GN_EPS = 64e-5
IN_SIZES = (MOBA_WIDTH, MOBA_WIDTH, MOBA_WIDTH, RWKV_SHIFT_WIDTH, 2 * D_MODEL)
IN_WIDTH = sum(IN_SIZES)
PEER_HEADS = 8
PEER_NKEYS = 128
PEER_EXPERTS = PEER_NKEYS * PEER_NKEYS
PEER_QDIM = 256
PEER_HALF = PEER_QDIM // 2
PEER_TOPK = 16
PEER_CHUNK = 128
RMS_EPS = 1e-6
NEG_INF = -1e30


def rms_norm(x, g, eps=RMS_EPS):
    x32 = x.astype(jnp.float32)
    y = x32 * lax.rsqrt(jnp.mean(x32 * x32, axis=-1, keepdims=True) + eps)
    return (y * g.astype(jnp.float32)).astype(x.dtype)

def rope_partial(x, pos):
    half = ROPE_DIM // 2
    inv = ROPE_THETA ** (-(jnp.arange(half, dtype=jnp.float32) * 2.0) / ROPE_DIM)
    ang = pos.astype(jnp.float32)[..., None] * inv
    cos = jnp.cos(ang)[:, :, None, :]
    sin = jnp.sin(ang)[:, :, None, :]
    x32 = x.astype(jnp.float32)
    x1 = x32[..., :half]
    x2 = x32[..., half:ROPE_DIM]
    out = jnp.concatenate([x1 * cos - x2 * sin, x2 * cos + x1 * sin, x32[..., ROPE_DIM:]], axis=-1)
    return out.astype(x.dtype)

def moba_attention(q, k, v):
    B, S, H, Dh = q.shape
    nb = -(-S // MOBA_BLOCK)
    sp = nb * MOBA_BLOCK
    pad = ((0, 0), (0, 0), (0, sp - S), (0, 0))
    q, k, v = (jnp.pad(t.transpose(0, 2, 1, 3), pad) for t in (q, k, v))
    kb = k.reshape(B, H, nb, MOBA_BLOCK, Dh)
    vb = v.reshape(B, H, nb, MOBA_BLOCK, Dh)
    scale = Dh ** -0.5
    qblk = jnp.arange(sp) // MOBA_BLOCK
    n_sel = min(MOBA_TOPK, nb - 1)
    if n_sel > 0:
        kmean = jnp.mean(kb.astype(jnp.float32), axis=3)
        gscore = jnp.einsum('bhsd,bhnd->bhsn', q.astype(jnp.float32), kmean)
        past = jnp.arange(nb)[None, :] < qblk[:, None]
        gscore = jnp.where(past, gscore, NEG_INF)
        _, sel = lax.top_k(gscore, n_sel)
        sel_ok = jnp.arange(n_sel)[None, :] < qblk[:, None]
    bi = jnp.arange(B)[:, None, None, None]
    hi = jnp.arange(H)[None, :, None, None]

    def attend_chunk(i):
        s0 = i * MOBA_Q_CHUNK
        qc = lax.dynamic_slice_in_dim(q, s0, MOBA_Q_CHUNK, axis=2)
        qpos = s0 + jnp.arange(MOBA_Q_CHUNK)
        own = s0 // MOBA_BLOCK
        k_own = lax.dynamic_index_in_dim(kb, own, axis=2, keepdims=False)
        v_own = lax.dynamic_index_in_dim(vb, own, axis=2, keepdims=False)
        kpos = own * MOBA_BLOCK + jnp.arange(MOBA_BLOCK)
        s_own = jnp.einsum('bhcd,bhkd->bhck', qc, k_own).astype(jnp.float32) * scale
        s_own = jnp.where(kpos[None, :] <= qpos[:, None], s_own, NEG_INF)
        if n_sel == 0:
            p = jax.nn.softmax(s_own, axis=-1).astype(v.dtype)
            return jnp.einsum('bhck,bhkd->bhcd', p, v_own)
        selc = lax.dynamic_slice_in_dim(sel, s0, MOBA_Q_CHUNK, axis=2)
        ok = lax.dynamic_slice_in_dim(sel_ok, s0, MOBA_Q_CHUNK, axis=0)
        k_sel = kb[bi, hi, selc]
        v_sel = vb[bi, hi, selc]
        s_sel = jnp.einsum('bhcd,bhcnkd->bhcnk', qc, k_sel).astype(jnp.float32) * scale
        s_sel = jnp.where(ok[None, None, :, :, None], s_sel, NEG_INF)
        s_all = jnp.concatenate([s_sel.reshape(B, H, MOBA_Q_CHUNK, n_sel * MOBA_BLOCK), s_own], axis=-1)
        p = jax.nn.softmax(s_all, axis=-1).astype(v.dtype)
        p_sel = p[..., :n_sel * MOBA_BLOCK].reshape(B, H, MOBA_Q_CHUNK, n_sel, MOBA_BLOCK)
        p_own = p[..., n_sel * MOBA_BLOCK:]
        return (jnp.einsum('bhcnk,bhcnkd->bhcd', p_sel, v_sel)
                + jnp.einsum('bhck,bhkd->bhcd', p_own, v_own))

    out = lax.map(attend_chunk, jnp.arange(sp // MOBA_Q_CHUNK))
    out = out.transpose(1, 0, 3, 2, 4).reshape(B, sp, H, Dh)
    return out[:, :S]

def token_shift(z, mu):
    prev = jnp.pad(z, ((0, 0), (1, 0), (0, 0)))[:, :-1]
    return z + (prev - z) * mu

def rwkv7_time_mix(zr, zk, zv, zw, za, zg, w0, w2, a0, a2, g2, k_k, k_a, r_k, ln_g, ln_b):
    B, S, _ = zr.shape
    H, N = RWKV_HEADS, HEAD_DIM
    f32 = jnp.float32
    w = -jax.nn.softplus(-(w0 + jnp.tanh(zw) @ w2)) - 0.5
    decay = jnp.exp(-jnp.exp(w.astype(f32)))
    a = jax.nn.sigmoid(a0 + za @ a2)
    g = jax.nn.sigmoid(zg) @ g2
    heads = lambda t: t.reshape(B, S, H, N).astype(f32)
    kk = heads(zk * k_k)
    kk = kk / jnp.maximum(jnp.sqrt(jnp.sum(kk * kk, axis=-1, keepdims=True)), 1e-12)
    k = zk * (1.0 + (a - 1.0) * k_a)
    r_h, k_h, v_h, a_h, d_h = heads(zr), heads(k), heads(zv), heads(a), heads(decay)

    def step(state, inp):
        r_t, d_t, k_t, v_t, kk_t, a_t = inp
        sa = jnp.einsum('bhij,bhj->bhi', state, -kk_t)
        state = (state * d_t[:, :, None, :] + sa[..., None] * (kk_t * a_t)[:, :, None, :]
                 + v_t[..., None] * k_t[:, :, None, :])
        return state, jnp.einsum('bhij,bhj->bhi', state, r_t)

    xs = tuple(t.transpose(1, 0, 2, 3) for t in (r_h, d_h, k_h, v_h, kk, a_h))
    _, y = lax.scan(step, jnp.zeros((B, H, N, N), f32), xs)
    y = y.transpose(1, 0, 2, 3)
    mean = jnp.mean(y, axis=-1, keepdims=True)
    var = jnp.mean(jnp.square(y - mean), axis=-1, keepdims=True)
    y = ((y - mean) * lax.rsqrt(var + GN_EPS)).reshape(B, S, H * N)
    y = y * ln_g.astype(f32) + ln_b.astype(f32)
    bonus = jnp.sum(r_h * k_h * r_k.astype(f32), axis=-1, keepdims=True) * v_h
    y = y + bonus.reshape(B, S, H * N)
    return (y * g.astype(f32)).astype(zr.dtype)

def peer_ffn(xn, wq, subkeys, u_tab, v_tab):
    B, S, D = xn.shape
    T = B * S
    xt = xn.reshape(T, D)
    q = (xt @ wq).reshape(T, PEER_HEADS, 2, PEER_HALF)
    s = jnp.einsum('thpd,hpnd->thpn', q, subkeys).astype(jnp.float32)
    top_s, top_i = lax.top_k(s, PEER_TOPK)
    cand_s = (top_s[:, :, 0, :, None] + top_s[:, :, 1, None, :]).reshape(T, PEER_HEADS, PEER_TOPK * PEER_TOPK)
    cand_i = (top_i[:, :, 0, :, None] * PEER_NKEYS + top_i[:, :, 1, None, :]).reshape(T, PEER_HEADS, PEER_TOPK * PEER_TOPK)
    best_s, best_j = lax.top_k(cand_s, PEER_TOPK)
    idx = jnp.take_along_axis(cand_i, best_j, axis=-1)
    gates = jax.nn.softmax(best_s, axis=-1)
    nc = T // PEER_CHUNK

    def retrieve(args):
        xc, ic, gc = args
        uc = u_tab[ic]
        vc = v_tab[ic]
        hdn = jax.nn.gelu(jnp.einsum('cd,chkd->chk', xc, uc).astype(jnp.float32), approximate=False) * gc
        return jnp.einsum('chk,chkd->cd', hdn.astype(vc.dtype), vc)

    out = lax.map(retrieve, (xt.reshape(nc, PEER_CHUNK, D),
                             idx.reshape(nc, PEER_CHUNK, PEER_HEADS, PEER_TOPK),
                             gates.reshape(nc, PEER_CHUNK, PEER_HEADS, PEER_TOPK)))
    return out.reshape(B, S, D).astype(xn.dtype)

def first_inputs(seed: int = 0) -> dict:
    key = jax.random.key(seed)
    ks = iter(jax.random.split(key, 40))
    L = DEPTH
    D = D_MODEL
    nrm = lambda shape, sc: jax.random.normal(next(ks), shape, jnp.float32) * sc
    unif = lambda shape, lo, hi: jax.random.uniform(next(ks), shape, jnp.float32, lo, hi)
    x = nrm((BATCH, SEQ, D), 1.0)
    c = nrm((BATCH, D), 1.0)
    positions = jnp.tile(jnp.arange(SEQ, dtype=jnp.int32)[None, :], (BATCH, 1))
    return {
        'x': x, 'c': c, 'positions': positions,
        'w_ada': nrm((L, D, 6 * D), 0.5 * D ** -0.5),
        'b_ada': nrm((L, 6 * D), 0.02),
        'norm1_g': 1.0 + nrm((L, D), 0.05),
        'w_in': nrm((L, D, IN_WIDTH), D ** -0.5),
        'q_norm_g': 1.0 + nrm((L, HEAD_DIM), 0.05),
        'k_norm_g': 1.0 + nrm((L, HEAD_DIM), 0.05),
        'rwkv_mu': unif((L, RWKV_SHIFT_WIDTH), 0.0, 1.0),
        'rwkv_w0': nrm((L, RWKV_WIDTH), 1.0) - 2.0,
        'rwkv_w2': nrm((L, RWKV_DECAY_LORA, RWKV_WIDTH), 0.5 * RWKV_DECAY_LORA ** -0.5),
        'rwkv_a0': nrm((L, RWKV_WIDTH), 0.5),
        'rwkv_a2': nrm((L, RWKV_AAA_LORA, RWKV_WIDTH), 0.5 * RWKV_AAA_LORA ** -0.5),
        'rwkv_g2': nrm((L, RWKV_GATE_LORA, RWKV_WIDTH), RWKV_GATE_LORA ** -0.5),
        'rwkv_k_k': 0.85 + nrm((L, RWKV_WIDTH), 0.1),
        'rwkv_k_a': 1.0 + nrm((L, RWKV_WIDTH), 0.1),
        'rwkv_r_k': nrm((L, RWKV_HEADS, HEAD_DIM), 0.1),
        'rwkv_ln_g': 1.0 + nrm((L, RWKV_WIDTH), 0.05),
        'rwkv_ln_b': nrm((L, RWKV_WIDTH), 0.02),
        'w_proj_moba': nrm((L, MOBA_WIDTH, D), MOBA_WIDTH ** -0.5),
        'w_proj_rwkv': nrm((L, RWKV_WIDTH, D), RWKV_WIDTH ** -0.5),
        'w_out': nrm((L, D, D), D ** -0.5),
        'norm2_g': 1.0 + nrm((L, D), 0.05),
        'peer_wq': nrm((L, D, PEER_HEADS * PEER_QDIM), D ** -0.5),
        'peer_subkeys': nrm((L, PEER_HEADS, 2, PEER_NKEYS, PEER_HALF), PEER_HALF ** -0.5),
        'peer_u': nrm((L, PEER_EXPERTS, D), D ** -0.5),
        'peer_v': nrm((L, PEER_EXPERTS, D), PEER_HEADS ** -0.5),
    }

def first_block(x, c, positions, w_ada, b_ada, norm1_g, w_in, q_norm_g, k_norm_g, rwkv_mu,
              rwkv_w0, rwkv_w2, rwkv_a0, rwkv_a2, rwkv_g2, rwkv_k_k, rwkv_k_a, rwkv_r_k,
              rwkv_ln_g, rwkv_ln_b, w_proj_moba, w_proj_rwkv, w_out, norm2_g, peer_wq,
              peer_subkeys, peer_u, peer_v):
    B, S, D = x.shape
    split_at = [int(v) for v in np.cumsum(IN_SIZES)[:-1]]
    rwkv_split = [int(v) for v in np.cumsum((RWKV_WIDTH, RWKV_WIDTH, RWKV_WIDTH, RWKV_DECAY_LORA, RWKV_AAA_LORA))]
    h = x
    for l in range(DEPTH):
        mod = (jax.nn.silu(c) @ w_ada[l] + b_ada[l])[:, None, :]
        sh1, sc1, gt1, sh2, sc2, gt2 = jnp.split(mod, 6, axis=-1)
        xn = rms_norm(h, norm1_g[l]) * (1.0 + sc1) + sh1
        proj = xn @ w_in[l]
        qm, km, vm, zrw, gate_logits = jnp.split(proj, split_at, axis=-1)
        qm = rope_partial(rms_norm(qm.reshape(B, S, MOBA_HEADS, HEAD_DIM), q_norm_g[l]), positions)
        km = rope_partial(rms_norm(km.reshape(B, S, MOBA_HEADS, HEAD_DIM), k_norm_g[l]), positions)
        vm = vm.reshape(B, S, MOBA_HEADS, HEAD_DIM)
        o_moba = moba_attention(qm, km, vm).reshape(B, S, MOBA_WIDTH)
        zrw = token_shift(zrw, rwkv_mu[l])
        zr, zk, zv, zw, za, zg = jnp.split(zrw, rwkv_split, axis=-1)
        o_rwkv = rwkv7_time_mix(zr, zk, zv, zw, za, zg, rwkv_w0[l], rwkv_w2[l], rwkv_a0[l],
                                rwkv_a2[l], rwkv_g2[l], rwkv_k_k[l], rwkv_k_a[l], rwkv_r_k[l],
                                rwkv_ln_g[l], rwkv_ln_b[l])
        g_moba, g_rwkv = jnp.split(jax.nn.sigmoid(gate_logits), 2, axis=-1)
        mixed = g_moba * (o_moba @ w_proj_moba[l]) + g_rwkv * (o_rwkv @ w_proj_rwkv[l])
        h = h + gt1 * (mixed @ w_out[l])
        xn2 = rms_norm(h, norm2_g[l]) * (1.0 + sc2) + sh2
        h = h + gt2 * peer_ffn(xn2, peer_wq[l], peer_subkeys[l], peer_u[l], peer_v[l])
    return h


DEPTH_2 = 2

N_A = DEPTH_2 // 2
N_B = DEPTH_2 - N_A

H_A = 4
DK_A = D_MODEL // H_A
DV_A = 2 * DK_A
WIDTH_A = H_A * DV_A
CHUNK = 128
ROPE_BASE_A = 10000.0

H_B = 16
QK_NOPE = 128
QK_ROPE = 64
V_HEAD = 128
Q_LORA = 768
KV_LORA = 512
WIDTH_B = H_B * V_HEAD
Q_BLOCK = 128
ROPE_BASE_B = 10000.0

IN_A = H_A * DK_A * 2 + WIDTH_A + WIDTH_A
IN_B = Q_LORA + WIDTH_B

DEEPNORM_ALPHA = (2.0 * DEPTH_2) ** 0.25
DEEPNORM_BETA = (8.0 * DEPTH_2) ** -0.25


def _layer_norm(x, g, b, eps=1e-5):
    xf = x.astype(jnp.float32)
    mu = jnp.mean(xf, axis=-1, keepdims=True)
    var = jnp.mean(jnp.square(xf - mu), axis=-1, keepdims=True)
    return ((xf - mu) * lax.rsqrt(var + eps)).astype(x.dtype) * g + b

def _rms_norm(x, g, eps=1e-6):
    xf = x.astype(jnp.float32)
    return (xf * lax.rsqrt(jnp.mean(jnp.square(xf), axis=-1, keepdims=True) + eps)).astype(x.dtype) * g

def _rope(x, base):
    s, d = x.shape[1], x.shape[-1]
    half = d // 2
    inv = base ** (-jnp.arange(half, dtype=jnp.float32) / half)
    ang = jnp.arange(s, dtype=jnp.float32)[:, None] * inv[None, :]
    shp = (s,) + (1,) * (x.ndim - 3) + (half,)
    cos = jnp.cos(ang).reshape(shp).astype(x.dtype)
    sin = jnp.sin(ang).reshape(shp).astype(x.dtype)
    x1, x2 = x[..., :half], x[..., half:]
    return jnp.concatenate([x1 * cos - x2 * sin, x2 * cos + x1 * sin], axis=-1)

def _chunkwise_retention(q, k, v):
    b, s, h, dk = q.shape
    dv = v.shape[-1]
    n = s // CHUNK

    def to_chunks(t):
        return t.astype(jnp.float32).reshape(b, n, CHUNK, h, t.shape[-1]).transpose(1, 0, 3, 2, 4)

    qc, kc, vc = to_chunks(q), to_chunks(k), to_chunks(v)
    lg = jnp.log1p(-jnp.exp2(-5.0 - jnp.arange(h, dtype=jnp.float32)))
    idx = jnp.arange(CHUNK, dtype=jnp.float32)
    diff = idx[:, None] - idx[None, :]
    causal = diff >= 0
    dmat = jnp.where(causal, jnp.exp(jnp.where(causal, diff, 0.0)[None] * lg[:, None, None]), 0.0)
    qdec = jnp.exp((idx + 1.0)[None, :] * lg[:, None])
    kdec = jnp.exp((CHUNK - 1.0 - idx)[None, :] * lg[:, None])
    cdec = jnp.exp(CHUNK * lg)

    def step(state, inp):
        qi, ki, vi = inp
        scores = jnp.einsum('bhcd,bhed->bhce', qi, ki) * dmat
        inner = jnp.einsum('bhce,bhev->bhcv', scores, vi)
        cross = jnp.einsum('bhcd,bhdv->bhcv', qi * qdec[None, :, :, None], state)
        state = state * cdec[None, :, None, None] + jnp.einsum(
            'bhcd,bhcv->bhdv', ki * kdec[None, :, :, None], vi)
        return state, inner + cross

    init = jnp.zeros((b, h, dk, dv), jnp.float32)
    _, out = lax.scan(step, init, (qc, kc, vc))
    return out.transpose(1, 0, 3, 2, 4).reshape(b, s, h, dv)

def _retention_layer(x, w_in, w_out):
    b, s, _ = x.shape
    hproj = x @ w_in
    qk = H_A * DK_A
    q = hproj[..., :qk].reshape(b, s, H_A, DK_A)
    k = hproj[..., qk:2 * qk].reshape(b, s, H_A, DK_A)
    v = hproj[..., 2 * qk:2 * qk + WIDTH_A].reshape(b, s, H_A, DV_A)
    gate = hproj[..., 2 * qk + WIDTH_A:]
    q = _rope(q, ROPE_BASE_A)
    k = _rope(k, ROPE_BASE_A) * (DK_A ** -0.5)
    o = _chunkwise_retention(q, k, v)
    mu = jnp.mean(o, axis=-1, keepdims=True)
    var = jnp.mean(jnp.square(o - mu), axis=-1, keepdims=True)
    o = ((o - mu) * lax.rsqrt(var + 1e-5)).astype(x.dtype).reshape(b, s, WIDTH_A)
    return (o * jax.nn.silu(gate)) @ w_out

def _shared_latent_kv(x, w_down, kv_norm, w_up):
    b, s, _ = x.shape
    c = x @ w_down
    lat = _rms_norm(c[..., :KV_LORA], kv_norm)
    k_rope = _rope(c[..., KV_LORA:], ROPE_BASE_B)
    kv = (lat @ w_up).reshape(b, s, H_B, QK_NOPE + V_HEAD)
    return kv[..., :QK_NOPE], k_rope, kv[..., QK_NOPE:]

def _causal_block_attention(q_nope, q_rope, k_nope, k_rope, v):
    b, s, h, _ = q_nope.shape
    nb = s // Q_BLOCK
    scale = (QK_NOPE + QK_ROPE) ** -0.5
    qn_b = q_nope.reshape(b, nb, Q_BLOCK, h, QK_NOPE).transpose(1, 0, 2, 3, 4)
    qr_b = q_rope.reshape(b, nb, Q_BLOCK, h, QK_ROPE).transpose(1, 0, 2, 3, 4)
    kpos = jnp.arange(s)

    def block(args):
        qn_i, qr_i, i = args
        sc = (jnp.einsum('bqhd,bkhd->bhqk', qn_i, k_nope)
              + jnp.einsum('bqhr,bkr->bhqk', qr_i, k_rope)).astype(jnp.float32) * scale
        qpos = i * Q_BLOCK + jnp.arange(Q_BLOCK)
        sc = jnp.where(kpos[None, :] <= qpos[:, None], sc, -jnp.inf)
        p = jax.nn.softmax(sc, axis=-1).astype(v.dtype)
        return jnp.einsum('bhqk,bkhd->bqhd', p, v)

    out = lax.map(block, (qn_b, qr_b, jnp.arange(nb)))
    return out.transpose(1, 0, 2, 3, 4).reshape(b, s, h, V_HEAD)

def _mla_layer(x, w_in, q_norm, w_uq, w_out, k_nope, k_rope, v):
    b, s, _ = x.shape
    hproj = x @ w_in
    q_lat, gate = hproj[..., :Q_LORA], hproj[..., Q_LORA:]
    q = (_rms_norm(q_lat, q_norm) @ w_uq).reshape(b, s, H_B, QK_NOPE + QK_ROPE)
    q_nope = q[..., :QK_NOPE]
    q_rope = _rope(q[..., QK_NOPE:], ROPE_BASE_B)
    o = _causal_block_attention(q_nope, q_rope, k_nope, k_rope, v).reshape(b, s, WIDTH_B)
    return (o * jax.nn.silu(gate)) @ w_out

def second_inputs(seed: int = 0) -> dict:
    key = jax.random.key(seed)
    ks = jax.random.split(key, 16)
    nrm = jax.random.normal
    f32 = jnp.float32
    return {
        "x": nrm(ks[0], (BATCH, SEQ, D_MODEL), f32),
        "a_w_in": nrm(ks[1], (N_A, D_MODEL, IN_A), f32) * D_MODEL ** -0.5,
        "a_w_out": nrm(ks[2], (N_A, WIDTH_A, D_MODEL), f32) * (WIDTH_A ** -0.5 * DEEPNORM_BETA),
        "b_w_in": nrm(ks[3], (N_B, D_MODEL, IN_B), f32) * D_MODEL ** -0.5,
        "b_q_norm": 1.0 + 0.02 * nrm(ks[4], (N_B, Q_LORA), f32),
        "b_w_uq": nrm(ks[5], (N_B, Q_LORA, H_B * (QK_NOPE + QK_ROPE)), f32) * Q_LORA ** -0.5,
        "b_w_out": nrm(ks[6], (N_B, WIDTH_B, D_MODEL), f32) * (WIDTH_B ** -0.5 * DEEPNORM_BETA),
        "kv_w_down": nrm(ks[7], (D_MODEL, KV_LORA + QK_ROPE), f32) * D_MODEL ** -0.5,
        "kv_norm": 1.0 + 0.02 * nrm(ks[8], (KV_LORA,), f32),
        "kv_w_up": nrm(ks[9], (KV_LORA, H_B * (QK_NOPE + V_HEAD)), f32) * KV_LORA ** -0.5,
        "ln_g": 1.0 + 0.02 * nrm(ks[10], (DEPTH_2, D_MODEL), f32),
        "ln_b": 0.02 * nrm(ks[11], (DEPTH_2, D_MODEL), f32),
    }

def second_block(x, a_w_in, a_w_out, b_w_in, b_q_norm, b_w_uq, b_w_out,
              kv_w_down, kv_norm, kv_w_up, ln_g, ln_b):
    shared = None
    for layer in range(DEPTH_2):
        if layer < N_A:
            y = _retention_layer(x, a_w_in[layer], a_w_out[layer])
        else:
            j = layer - N_A
            if j == 0:
                shared = _shared_latent_kv(x, kv_w_down, kv_norm, kv_w_up)
            y = _mla_layer(x, b_w_in[j], b_q_norm[j], b_w_uq[j], b_w_out[j], *shared)
        x = _layer_norm(DEEPNORM_ALPHA * x + y, ln_g[layer], ln_b[layer])
    return x


def setup_inputs(seed=0):
    out = dict(first_inputs(seed))
    for name, value in second_inputs(seed + 1).items():
        if name != "x":
            out[name + "_2"] = value
    return out


def reference(
    x, c, positions, w_ada, b_ada, norm1_g, w_in, q_norm_g, k_norm_g, rwkv_mu, rwkv_w0, rwkv_w2,
    rwkv_a0, rwkv_a2, rwkv_g2, rwkv_k_k, rwkv_k_a, rwkv_r_k, rwkv_ln_g, rwkv_ln_b, w_proj_moba,
    w_proj_rwkv, w_out, norm2_g, peer_wq, peer_subkeys, peer_u, peer_v, a_w_in_2, a_w_out_2,
    b_w_in_2, b_q_norm_2, b_w_uq_2, b_w_out_2, kv_w_down_2, kv_norm_2, kv_w_up_2, ln_g_2,
    ln_b_2,
):
    x = first_block(
        x, c, positions, w_ada, b_ada, norm1_g, w_in, q_norm_g, k_norm_g, rwkv_mu, rwkv_w0,
        rwkv_w2, rwkv_a0, rwkv_a2, rwkv_g2, rwkv_k_k, rwkv_k_a, rwkv_r_k, rwkv_ln_g, rwkv_ln_b,
        w_proj_moba, w_proj_rwkv, w_out, norm2_g, peer_wq, peer_subkeys, peer_u, peer_v,
    )
    return second_block(
        x, a_w_in_2, a_w_out_2, b_w_in_2, b_q_norm_2, b_w_uq_2, b_w_out_2, kv_w_down_2,
        kv_norm_2, kv_w_up_2, ln_g_2, ln_b_2,
    )


_drawn_inputs = setup_inputs


def setup_inputs(seed=0):
    import zlib

    import numpy as np

    out = dict(_drawn_inputs(seed))
    spreads = {}
    factors = {'b_ada': 3.608,
     'norm1_g': 5.059,
     'q_norm_g': 8.0,
     'k_norm_g': 8.0,
     'rwkv_w2': 6.539,
     'rwkv_k_k': 7.695,
     'rwkv_k_a': 4.041,
     'rwkv_ln_g': 8.0,
     'rwkv_ln_b': 32.715,
     'norm2_g': 3.908,
     'b_q_norm_2': 8.0,
     'kv_norm_2': 8.0}
    for name, (base, spread) in spreads.items():
        noise = np.random.default_rng([zlib.crc32(name.encode()), seed]).standard_normal(out[name].shape)
        drawn = base * np.exp(spread * noise) if base else spread * noise
        out[name] = __import__('jax').numpy.asarray(drawn.astype(out[name].dtype))
    for name, factor in factors.items():
        out[name] = (out[name] * factor).astype(out[name].dtype)
    return out
```

```python
import concourse.bass as bass
from concourse import mybir
from concourse.alu_op_type import AluOpType as ALU
from contextlib import ExitStack
import numpy as np

F32 = mybir.dt.float32
I32 = mybir.dt.int32
U32 = mybir.dt.uint32
ACT = mybir.ActivationFunctionType
AX = mybir.AxisListType
P = 128
T = 256
NEG = -1e30
PI = float(np.pi)

C1 = {}
_o = 0
for _n, _w in (("ident", 128), ("ones", 128), ("blk", 128), ("rotA", 128), ("rotB", 128), ("mXd", 128),
               ("mXo", 128), ("mYd", 128), ("m32s", 128), ("m32i", 128), ("mask3", 384), ("reset", 256),
               ("iota", 128), ("inv", 1), ("pad", 3)):
    C1[_n] = (_o, _w)
    _o += _w
C1W = _o
C2 = {"cosA": (0, 256), "sinA": (256, 256), "cosB": (512, 256), "sinB": (768, 256), "dec": (1024, 1536)}
C2W = 2560
VEC = {}
_o = 0
for _n, _w in (("c", 8), ("b_ada", 48), ("n1", 8), ("n2", 8), ("qg", 1), ("kg", 1), ("mu", 14), ("w0", 4),
               ("a0", 4), ("k_k", 4), ("k_a", 4), ("r_k", 4), ("ln_g", 4), ("ln_b", 4), ("bq", 6), ("kvn", 4),
               ("g2", 16), ("b2", 16)):
    VEC[_n] = (_o, _w)
    _o += _w
VECW = _o

WEIGHTS = {
    "ada": (8, 4, 12), "in_wag": (8, 2, 1), "in_rkv": (8, 4, 3), "in_v": (8, 4, 1), "in_qk": (8, 4, 2),
    "in_g": (8, 4, 4), "pm": (4, 8, 1), "pr": (4, 8, 1), "wo": (8, 4, 2), "wq": (8, 4, 4), "sub": (1, 16, 1),
    "u": (8, 4, 32), "v": (4, 8, 32),
    "a_qk": (8, 4, 4), "a_v": (8, 4, 4), "a_g": (8, 4, 4), "a_o": (16, 2, 4),
    "kvd": (8, 4, 1), "kvr": (8, 1, 1), "kvk": (4, 8, 2), "kvv": (4, 8, 2),
    "b_q4": (8, 4, 1), "b_q2": (8, 2, 1), "b_g": (8, 4, 4), "uqn": (6, 4, 4), "uqr": (6, 4, 2), "b_o": (16, 2, 4),
}
NSLOT = 4
SLOT = 4096
ARENA = 30380


class Queue:

    def __init__(self, sem, chained):
        self.sem, self.chained = sem, chained
        self.n = 0
        self.items = []
        self.met = {}

    def wait(self, *toks):
        for t in toks:
            if t is None:
                continue
            if isinstance(t, list):
                self.wait(*t)
                continue
            sem, v = t
            if v > self.met.get(id(sem), 0):
                self.met[id(sem)] = v
                self.items.append((None, sem, v))

    def add(self, fn, *toks, signal=True):
        if self.chained and self.n:
            self.wait((self.sem, self.n))
        self.wait(*toks)
        if not signal:
            self.items.append((fn, None, 0))
            return None
        self.n += 1
        self.items.append((fn, self.sem, 1))
        return (self.sem, self.n)

    def last(self):
        return (self.sem, self.n)

    def run(self, eng):
        for fn, sem, v in self.items:
            if fn is None:
                eng.wait_ge(sem, v)
            elif sem is None:
                fn(eng)
            else:
                fn(eng).then_inc(sem, v)


class Bank:

    def __init__(self, ap):
        self.ap = ap
        self.free = []


class Buf:

    def __init__(self, aps):
        self.slots = [Bank(a) for a in aps]
        self.i = -1

    def next(self):
        self.i = (self.i + 1) % len(self.slots)
        return self.slots[self.i]


class Arena:
    def __init__(self, t, lo, hi):
        self.t, self.at, self.hi = t, lo, hi

    def take(self, n):
        o = self.at
        self.at += n
        assert self.at <= self.hi, (self.at, self.hi)
        return self.t[:, o:o + n]

    def tiles(self, k, n=T):
        return self.take(k * n).rearrange("p (k t) -> p k t", k=k)


def build_program(nc, D, out, stop=None, dumps=None):
    ctx = ExitStack()
    with ctx:
        def sbuf(name, shape, dt=F32):
            return ctx.enter_context(nc.sbuf_tensor(name, shape, dt))

        def sem(name):
            return ctx.enter_context(nc.semaphore(name))

        ring = sbuf("ring", [P, NSLOT * SLOT])
        con = sbuf("con", [P, C1W])
        vec = sbuf("vec", [P, VECW])
        mod = sbuf("mod", [P, 64])
        small = sbuf("small", [P, 64])
        Xt = sbuf("Xt", [P, 8 * T])
        XNt = sbuf("XNt", [P, 8 * T])
        ar = sbuf("ar", [P, ARENA])
        X = Xt[:, :].rearrange("p (k t) -> p k t", k=8)
        XN = XNt[:, :].rearrange("p (k t) -> p k t", k=8)
        banks = [Bank(ctx.enter_context(nc.psum_tensor(f"ps{i}", [P, 512], F32))[:, :]) for i in range(8)]

        pe = Queue(sem("s_pe"), False)
        ve = Queue(sem("s_ve"), True)
        ac = Queue(sem("s_ac"), True)
        po = Queue(sem("s_po"), True)
        sp = Queue(sem("s_sp"), False)
        slot_sem = [sem(f"s_w{i}") for i in range(NSLOT)]
        s_ld = sem("s_ld")
        s_ldx = sem("s_ldx")
        s_ld2 = sem("s_ld2")
        s_out = sem("s_out")

        def cst(name, lo=0, hi=None):
            o, w = C1[name]
            return con[:, o + lo:o + (w if hi is None else hi)]

        def vc(name, i=0, n=1):
            o, _ = VEC[name]
            return vec[:, o + i:o + i + n]

        ident, ones, blk = cst("ident"), cst("ones"), cst("blk")

        def TT(o, a, b, op, *w, q=ve):
            return q.add(lambda e: e.tensor_tensor(o, a, b, op), *w)

        def TS(o, a, s1, s2, op0, op1, *w, q=ve):
            if s2 is None:
                return q.add(lambda e: e.tensor_scalar(o, a, s1, None, op0), *w)
            return q.add(lambda e: e.tensor_scalar(o, a, s1, s2, op0, op1), *w)

        def STT(o, a, s, b, op0, op1, *w):
            return ve.add(lambda e: e.scalar_tensor_tensor(o, a, s, b, op0, op1), *w)

        def CP(o, a, *w, q=ve):
            return q.add(lambda e: e.tensor_copy(o, a), *w)

        def AC(o, a, f, *w, **k):
            return ac.add(lambda e: e.activation(o, a, f, **k), *w)

        def REC(o, a, *w):
            return ve.add(lambda e: e.reciprocal(o, a), *w)

        pool_banks = [list(range(8)), 0]

        def bank():
            ids, i = pool_banks
            pool_banks[1] = (i + 1) % len(ids)
            b = banks[ids[i % len(ids)]]
            pe.wait(b.free)
            b.free = []
            return b

        def mm(o, pairs, *w, start=True, stop=True, signal=True, skip=False):
            pe.wait(*w)
            tok = None
            for i, (l, r) in enumerate(pairs):
                last = i == len(pairs) - 1
                tok = pe.add(lambda e, l=l, r=r, s=(start and i == 0), t=(stop and last):
                             e.matmul(o, l, r, start=s, stop=t, skip_group_check=skip),
                             signal=signal and last)
            return tok

        def tr(o, a, signal=True):
            return pe.add(lambda e: e.transpose(o, a, ident), signal=signal)

        chunks = []

        class Chunk:
            pass

        def chunk(name, j):
            kt, nf, _ = WEIGHTS[name]
            c = Chunk()
            c.name, c.j, c.idx, c.w = name, j, len(chunks), kt * nf * P
            s = c.idx % NSLOT
            c.flat = ring[:, s * SLOT:s * SLOT + c.w]
            c.ap = c.flat.rearrange("p (k f) -> p k f", k=kt)
            c.tok = (slot_sem[s], 16 * (c.idx // NSLOT + 1))
            c.done = None
            c.kt, c.nf = kt, nf
            chunks.append(c)
            return c

        def proj(name, x, consume, *w, j0=0, j1=None):
            kt, nf, nch = WEIGHTS[name]
            for j in range(j0, nch if j1 is None else j1):
                c = chunk(name, j)
                pe.wait(c.tok, *w)
                for f in range(0, nf, 2):
                    n = min(2, nf - f)
                    b = bank()
                    bv = b.ap[:, 0:n * T].rearrange("p (n t) -> p n t", n=n)
                    for g in range(n):
                        tok = mm(bv[:, g, :], [(c.ap[:, k, (f + g) * P:(f + g + 1) * P], x[:, k, :])
                                               for k in range(kt)], signal=g == n - 1)
                    c.done = tok
                    b.free = [consume(bv, j * nf + f, n, tok)]

        def proj_tok(name, x, consume, *w):
            kt, nf, nch = WEIGHTS[name]
            for j in range(nch):
                c = chunk(name, j)
                pe.wait(c.tok, *w)
                for f in range(0, nf * P, 512):
                    for tt in range(2):
                        b = bank()
                        tok = mm(b.ap, [(x[:, k, tt * P:(tt + 1) * P], c.ap[:, k, f:f + 512]) for k in range(kt)])
                        c.done = tok
                        b.free = [consume(b.ap, tt, j * nf * P + f, tok)]

        def barrier():
            toks = [q.last() for q in (pe, ve, ac, po) if q.n]
            for q in (pe, ve, ac, po):
                q.wait(toks)

        class Stop(Exception):
            pass

        def dump(name, ap):
            if dumps is not None and name in dumps:
                barrier()
                toks = [q.last() for q in (pe, ve, ac, po) if q.n]
                po.wait(toks)
                s = sem("s_d_" + name)
                po.add(lambda e: e.dma_start(dumps[name], ap).then_inc(s, 16), signal=False)
                po.wait((s, 16))
            if stop == name:
                raise Stop

        def rstd_of(o, src, scale, eps, *w):
            TS(o, src, scale, eps, ALU.mult, ALU.add, *w)
            t = REC(o, o)
            return AC(o, o, ACT.Sqrt, t)

        def colsum(x, nk, *w):
            b = bank()
            return b, mm(b.ap[:, 0:T], [(ones, x[:, k, :]) for k in range(nk)], *w)

        def bc(ap, n):
            return ap.unsqueeze(1).broadcast_to([P, n, T])

        ac.add(lambda e: e.dma_start(Xt[:, :], D["xT"]).then_inc(s_ldx, 16), signal=False)
        ac.add(lambda e: e.dma_start(vec[:, :], D["vec"]).then_inc(s_ldx, 16), signal=False)
        ac.add(lambda e: e.dma_start(con[:, :], D["con"]).then_inc(s_ldx, 16), signal=False)
        LDX = (s_ldx, 48)
        A = Arena(ar, 0, ARENA)
        lw = A.take(1024)
        posi = A.take(T)
        ac.add(lambda e: e.dma_start(lw[:, 0:512], D["w2a2"]).then_inc(s_ld, 16), signal=False)
        ac.add(lambda e: e.dma_start(lw[:, 512:1024], D["g2"]).then_inc(s_ld, 16), signal=False)
        ac.add(lambda e: e.dma_start(posi.bitcast(I32), D["pos"]).then_inc(s_ld, 16), signal=False)
        LD = (s_ld, 48)

        def stages():
            def ada(j0, j1, *w):
                b = bank()
                for j in range(j0, j1):
                    c = chunk("ada", j)
                    pe.wait(c.tok, *w)
                    for f in range(4):
                        col = 4 * j + f
                        c.done = mm(b.ap[:, col:col + 1], [(c.ap[:, k, f * P:(f + 1) * P], small[:, k:k + 1])
                                                           for k in range(8)], signal=f == 3)
                lo, hi = 4 * j0, 4 * j1
                t = TT(mod[:, lo:hi], b.ap[:, lo:hi], vc("b_ada", lo, hi - lo), ALU.add, chunks[-1].done)
                b.free = [t]
                return t

            sq = A.tiles(8)
            rs = A.take(T)
            t = AC(small[:, 8:16], vc("c", 0, 8), ACT.Sigmoid, LDX)
            t_c = TT(small[:, 0:8], vc("c", 0, 8), small[:, 8:16], ALU.mult, t, LDX)
            t = AC(sq, X, ACT.Square)
            b, t = colsum(sq, 8, t)
            t_r = rstd_of(rs, b.ap[:, 0:T], 1.0 / 1024, 1e-6, t)
            b.free = [ve.last()]
            TT(sq, X, bc(rs, 8), ALU.mult, t_r)
            t = ada(0, 4, t_c)
            STT(mod[:, 48:56], mod[:, 8:16], 1.0, vc("n1", 0, 8), ALU.add, ALU.mult)
            for k in range(8):
                t_xn = TS(XN[:, k, :], sq[:, k, :], mod[:, 48 + k:49 + k], mod[:, k:k + 1], ALU.mult, ALU.add)
            dump("xn", XN)

            cA, sA, tmpr = A.take(T), A.take(T), A.take(T)
            CP(cA, posi.bitcast(I32), LD)
            TS(cA, cA, cst("inv"), None, ALU.mult, None)
            TS(tmpr, cA, float(1 / (2 * np.pi)), 12582912.0, ALU.mult, ALU.add)
            TS(tmpr, tmpr, 12582912.0, None, ALU.subtract, None)
            c1 = 6.28125
            c2 = float(np.float32(2 * np.pi - c1))
            c3 = float(2 * np.pi - c1 - c2)
            for cc in (c1, c2, c3):
                STT(cA, tmpr, -cc, cA, ALU.mult, ALU.add)
            t = TS(cA, cA, PI, -PI, ALU.min, ALU.max)
            t = AC(sA, cA, ACT.Sin, t)
            t = AC(cA, cA, ACT.Abs)
            t = TS(cA, cA, -1.0, PI / 2, ALU.mult, ALU.add, t)
            t_rope = AC(cA, cA, ACT.Sin, t)

            z_at = A.at
            Z = A.tiles(14)
            ztr = Buf([A.take(2 * 257).rearrange("p (n t) -> p n t", n=2) for _ in range(2)])
            Gt = ar[:, z_at:z_at + 4096].rearrange("p (k t) -> p k t", k=16)
            assert A.at - z_at >= 4096
            zd = A.tiles(2)
            for s in ztr.slots:
                s.free = [ve.add(lambda e, s=s: e.memset(s.ap[:, :, 0:1], 0.0))]

            def shifted(first):
                def consume(bv, f, n, tok):
                    s = ztr.next()
                    t = AC(s.ap[:, :, 1:257], bv, ACT.Copy, tok, s.free)
                    TT(zd, s.ap[:, :, 0:256], s.ap[:, :, 1:257], ALU.subtract, t)
                    for g in range(2):
                        z = first + f + g
                        t2 = STT(Z[:, z, :], zd[:, g, :], vc("mu", z), s.ap[:, g, 1:257], ALU.mult, ALU.add)
                    s.free = [t2]
                    return t
                return consume

            proj("in_wag", XN, shifted(0), t_xn)
            proj("in_rkv", XN, shifted(2))
            t_z = ve.last()
            zr, zk, zv = Z[:, 2:6, :], Z[:, 6:10, :], Z[:, 10:14, :]
            Vt = A.take(1024).rearrange("p (t f) -> p t f", t=2)
            qk = A.tiles(8)

            def ev_v(bv, tt, f, tok):
                return AC(Vt[:, tt, f:f + 512], bv, ACT.Copy, tok)

            def ev_qk(bv, f, n, tok):
                return AC(qk[:, f:f + 2, :], bv, ACT.Copy, tok)

            def ev_g(bv, f, n, tok):
                return AC(Gt[:, f:f + 2, :], bv, ACT.Sigmoid, tok)

            proj_tok("in_v", XN, ev_v)
            proj("in_qk", XN, ev_qk)
            t_mod = ada(4, 12)
            dump("z", Z)

            t = AC(Z[0:64, 0, :], Z[0:64, 0, :], ACT.Tanh, t_z)
            t_w = t
            t_g = AC(Z[:, 1, :], Z[:, 1, :], ACT.Sigmoid)
            LDc, Aa, Gg = A.tiles(4), A.tiles(4), A.tiles(4)
            pe.wait(LD)
            for dst, lo, hi, z, off, bias in ((LDc, 0, 64, 0, 0, "w0"), (Aa, 64, 128, 0, 0, "a0"), (Gg, 0, 128, 1, 512, None)):
                for f in range(0, 4, 2):
                    b = bank()
                    for g in range(2):
                        tok = mm(b.ap[:, g * T:(g + 1) * T],
                                 [(lw[lo:hi, off + (f + g) * P:off + (f + g + 1) * P], Z[lo:hi, z, :])], t_w, t_g)
                    for g in range(2):
                        if bias:
                            b.free = [AC(dst[:, f + g, :], b.ap[:, g * T:(g + 1) * T], ACT.Sigmoid, tok,
                                         bias=vc(bias, f + g))]
                        else:
                            b.free = [AC(dst[:, f + g, :], b.ap[:, g * T:(g + 1) * T], ACT.Copy, tok)]
            t_lora = ac.last()
            Lc, EL, EmL, EP = A.tiles(4), A.tiles(4), A.tiles(4), A.tiles(4)
            TS(LDc, LDc, -float(np.exp(-0.5)), None, ALU.mult, None, t_lora)
            for k in range(4):
                ve.add(lambda e, k=k: e.tensor_tensor_scan(Lc[:, k, :], cst("reset"), LDc[:, k, :], 0.0,
                                                           ALU.mult, ALU.add))
            t = TT(EP, Lc, LDc, ALU.subtract)
            AC(EL, Lc, ACT.Exp, t)
            AC(EmL, Lc, ACT.Exp, scale=-1.0)
            t_e = AC(EP, EP, ACT.Exp)
            KK, Kt = A.tiles(4), A.tiles(4)
            bt_at = A.at
            Bt, tmp = A.tiles(4), Lc
            for k in range(4):
                TS(KK[:, k, :], zk[:, k, :], vc("k_k", k), None, ALU.mult, None)
            t = AC(tmp, KK, ACT.Square, ve.last())

            def blksum(src, o, scale, t):
                s2 = src.rearrange("p k t -> p (k t)")
                o2 = o.rearrange("p k t -> p (k t)")
                for f in range(2):
                    b = bank()
                    tk = mm(b.ap, [(blk, s2[:, f * 512:(f + 1) * 512])], t)
                    b.free = [TS(o2[:, f * 512:(f + 1) * 512], b.ap, scale, None, ALU.mult, None, tk)]
                return ve.last()

            RS4 = A.tiles(4)
            blksum(tmp, RS4, 1.0, t)
            t = TS(RS4, RS4, 1e-24, None, ALU.max, None)
            t = AC(RS4, RS4, ACT.Sqrt, t)
            REC(RS4, RS4, t)
            TT(KK, KK, RS4, ALU.mult)
            TS(small[:, 16:20], vc("k_a", 0, 4), -1.0, 1.0, ALU.mult, ALU.add)
            for k in range(4):
                TS(tmp[:, k, :], Aa[:, k, :], vc("k_a", k), small[:, 16 + k:17 + k], ALU.mult, ALU.add)
            TT(Kt, zk, tmp, ALU.mult)
            TT(Bt, KK, Aa, ALU.mult)
            for k in range(4):
                t = STT(tmp[:, k, :], zr[:, k, :], vc("r_k", k), Kt[:, k, :], ALU.mult, ALU.mult)
            BON = Aa
            t = blksum(tmp, BON, 1.0, t)
            TT(BON, BON, zv, ALU.mult)
            al, be, kd, rd = EP, EmL, Kt, zr
            STT(al, KK, -1.0, EP, ALU.mult, ALU.mult, t_e)
            TT(kd, Kt, EmL, ALU.mult)
            TT(be, Bt, EmL, ALU.mult)
            t_rw = TT(rd, zr, EL, ALU.mult)
            dump("al", al)

            SQ8 = A.tiles(4)
            qkf = A.tiles(8)
            for i, g in ((0, "qg"), (1, "kg")):
                v4 = qk[:, 4 * i:4 * i + 4, :]
                o4 = qkf[:, 4 * i:4 * i + 4, :]
                t = AC(SQ8, v4, ACT.Square, ve.last(), pe.last())
                blksum(SQ8, RS4, 1.0 / 64, t)
                TS(RS4, RS4, 1e-6, None, ALU.add, None)
                t = REC(RS4, RS4)
                t = AC(RS4, RS4, ACT.Sqrt, t)
                t = STT(v4, v4, vc(g), RS4, ALU.mult, ALU.mult, t)
                TT(o4, v4, bc(cA, 4), ALU.mult, t_rope)
                for f in range(0, 4, 2):
                    b = bank()
                    tk = mm(b.ap, [(cst("rotA"), qk[:, 4 * i + f:4 * i + f + 2, :])], t)
                    t2 = TT(SQ8[:, f:f + 2, :], b.ap.rearrange("p (n t) -> p n t", n=2), bc(sA, 2), ALU.mult, tk)
                    b.free = [t2]
                t_qk = TT(o4, o4, SQ8, ALU.add)
            Om = qk[:, 0:4, :]
            dump("qkf", qkf)

            def attention(mem, heads, dv, scale, parts, vof, base, evac, *w):
                sc = Buf([mem.take(384) for _ in range(3)])
                pt = Buf([mem.take(384) for _ in range(2)])
                st = {}

                def scores(h):
                    b = bank()
                    pe.wait(*w)
                    pr = parts(h)
                    mm(b.ap[:, 0:128], [(q[:, 0:128], k[:, 0:128]) for q, k in pr], signal=False)
                    tok = mm(b.ap[:, 128:384], [(q[:, 128:256], k[:, 0:256]) for q, k in pr])
                    s = sc.next()
                    STT(s.ap, b.ap[:, 0:384], scale, cst("mask3"), ALU.mult, ALU.add, tok, s.free)
                    b.free = [ve.last()]
                    n = small[:, 20 + 4 * (h % 4):24 + 4 * (h % 4)]
                    ve.add(lambda e: e.reduce_max(n[:, 0:1], s.ap[:, 0:128], AX.X, negate=True))
                    t = ve.add(lambda e: e.reduce_max(n[:, 1:2], s.ap[:, 128:384], AX.X, negate=True))
                    AC(s.ap[:, 0:128], s.ap[:, 0:128], ACT.Exp, t, bias=n[:, 0:1], accum_out=n[:, 2:3])
                    t = AC(s.ap[:, 128:384], s.ap[:, 128:384], ACT.Exp, bias=n[:, 1:2], accum_out=n[:, 3:4])
                    st[h] = (s, n, t)

                def weights(h):
                    s, n, t = st[h]
                    REC(n[:, 2:4], n[:, 2:4], t)
                    TS(s.ap[:, 0:128], s.ap[:, 0:128], n[:, 2:3], None, ALU.mult, None)
                    t = TS(s.ap[:, 128:384], s.ap[:, 128:384], n[:, 3:4], None, ALU.mult, None)
                    b = bank()
                    pe.wait(t)
                    for i in range(3):
                        tok = tr(b.ap[:, i * P:(i + 1) * P], s.ap[:, i * P:(i + 1) * P], signal=i == 2)
                    s.free = [tok]
                    p = pt.next()
                    t = AC(p.ap, b.ap[:, 0:384], ACT.Copy, tok, p.free)
                    b.free = [t]
                    st[h] = (p, t)

                def values(h):
                    p, t = st[h]
                    b = bank()
                    o = base(h)
                    mm(b.ap[o:o + dv, 0:256], [(vof(h, 0), p.ap[:, 0:256])], t, stop=False, signal=False)
                    tok = mm(b.ap[o:o + dv, 128:256], [(vof(h, 1), p.ap[:, 256:384])], start=False)
                    p.free = [tok]
                    b.free = [evac(h, b.ap[o:o + dv, 0:256], tok)]

                for i in range(heads + 2):
                    if i < heads:
                        scores(i)
                    if 1 <= i <= heads:
                        weights(i - 1)
                    if i >= 2:
                        values(i - 2)

            def head(a, h):
                return a[64 * (h % 2):64 * (h % 2) + 64, h // 2, :]

            attention(A, 8, 64, 0.125, lambda h: [(head(qkf[:, 0:4, :], h), head(qkf[:, 4:8, :], h))],
                      lambda h, kt: Vt[:, kt, 64 * h:64 * h + 64], lambda h: 64 * (h % 2),
                      lambda h, b, tok: AC(head(Om, h), b, ACT.Copy, tok, t_qk), t_qk)
            t_om = ac.last()
            dump("om", Om)

            barrier()
            B = Arena(ar, 0, ARENA)
            free = [ar[:, bt_at:ARENA], ar[:, 0:z_at]] + [x.rearrange("p k t -> p (k t)") for x in (KK, Lc, LDc, zk, Vt, qk[:, 4:8, :])]
            used = [0] * len(free)

            def grab(n):
                for i, f in enumerate(free):
                    if f.shape[1] - used[i] >= n:
                        o = used[i]
                        used[i] += n
                        return f[:, o:o + n]
                raise ValueError(n)

            def grab4():
                return grab(512).rearrange("p (q t) -> p q t", q=4)

            ST = grab(2048).rearrange("p (c k i) -> p c k i", c=8, k=4)
            AR_ = [grab4() for _ in range(4)]
            Yy = grab(1024).rearrange("p (k t) -> p k t", k=4)
            toks4 = {}
            for nm, src in (("al", al), ("be", be), ("kd", kd), ("v", zv)):
                d = grab(1024).rearrange("p (h f) -> p h f", h=2)
                for h in range(2):
                    b = bank()
                    pe.wait(t_rw)
                    for k in range(4):
                        tok = tr(b.ap[:, k * P:(k + 1) * P], src[:, k, h * P:(h + 1) * P], signal=k == 3)
                    b.free = [AC(d[:, h, :], b.ap, ACT.Copy, tok)]
                toks4[nm] = d
            t_tok = ac.last()
            alT, beT, kdT, vT = (toks4[n] for n in ("al", "be", "kd", "v"))
            U0 = grab(1024).rearrange("p (h a k i) -> p h a k i", h=2, a=2, k=4)
            U = U0
            WT = grab(1024).rearrange("p (k t) -> p k t", k=4)
            Xd, Xo, Yd, X2, Y2, X4, Y4, R, Rn, Yk = (grab4() for _ in range(10))
            AK = grab4()
            XV = grab(256).rearrange("p (q i) -> p q i", q=4)

            def b4(b):
                return b.ap.rearrange("p (q t) -> p q t", q=4)

            def m4(name):
                return cst(name).unsqueeze(1).broadcast_to([P, 4, P])

            def quad(ls, rs, *w):
                b = bank()
                pe.wait(*w)
                for k in range(4):
                    tok = mm(b4(b)[:, k, :], [(ls(k), rs(k))], signal=k == 3)
                return b, tok

            for g in range(4):
                hf, par = g // 2, g % 2
                lo, ts = 64 * par, slice(hf * P, hf * P + P)

                def sl(a):
                    return lambda k: a[lo:lo + 64, k, ts]

                def al4(a):
                    return lambda k: a[:, k, :]

                b, tk = quad(sl(al), sl(be), t_rw)
                TT(Xd, b4(b), m4("mXd"), ALU.mult, tk, pe.last())
                b.free = [TT(Xo, b4(b), m4("mXo"), ALU.mult)]
                b, tk = quad(sl(be), sl(al))
                b.free = [TT(Yd, b4(b), m4("mYd"), ALU.mult, tk)]
                b, tk = quad(sl(kd), sl(al))
                b.free = [TT(Yk, b4(b), m4("m32s"), ALU.mult, tk)]
                b, tk = quad(sl(be), sl(rd))
                b.free = [TT(AR_[g], b4(b), m4("m32i"), ALU.mult, tk)]
                b, tk = quad(sl(kd), sl(rd))
                b.free = [TT(AK, b4(b), m4("m32i"), ALU.mult, tk)]
                t = ve.last()
                b = bank()
                pe.wait(t, t_tok)
                for k in range(4):
                    tk = mm(b4(b)[lo:lo + 64, k, :], [(vT[:, hf, k * P + lo:k * P + lo + 64], AK[:, k, :])],
                            signal=k == 3)
                b.free = [AC(Yy[lo:lo + 64, :, ts], b4(b)[lo:lo + 64, :, :], ACT.Copy, tk)]
                t = TT(R, Yd, m4("ident"), ALU.add)
                b, tk = quad(al4(Yd), al4(Xd), t)
                b.free = [AC(X2, b4(b), ACT.Copy, tk)]
                b, tk = quad(al4(Xd), al4(Yd))
                b.free = [AC(Y2, b4(b), ACT.Copy, tk)]
                t = ac.last()
                b, tk = quad(al4(X2), al4(R), t)
                b.free = [TT(Rn, b4(b), R, ALU.add, tk)]
                tR = ve.last()
                b, tk = quad(al4(Y2), al4(X2))
                b.free = [AC(X4, b4(b), ACT.Copy, tk)]
                b, tk = quad(al4(X2), al4(Y2))
                b.free = [AC(Y4, b4(b), ACT.Copy, tk)]
                t = ac.last()
                b, tk = quad(al4(X4), al4(Rn), t, tR)
                b.free = [TT(R, b4(b), Rn, ALU.add, tk)]
                tR = ve.last()
                b, tk = quad(al4(Y4), al4(X4))
                b.free = [AC(X2, b4(b), ACT.Copy, tk)]
                t = ac.last()
                b, tk = quad(al4(X2), al4(R), t, tR)
                b.free = [TT(Rn, b4(b), R, ALU.add, tk)]
                tR = ve.last()
                b = bank()
                pe.wait(tR)
                for k in range(4):
                    tk = tr(b4(b)[:, k, :], Rn[:, k, :], signal=k == 3)
                b.free = [AC(X4, b4(b), ACT.Copy, tk)]
                b, tk = quad(al4(Xo), al4(Rn))
                b.free = [AC(Y4, b4(b), ACT.Copy, tk)]
                b, tk = quad(al4(X4), al4(Y4), ac.last())
                b.free = [TT(R, b4(b), Rn, ALU.add, tk)]
                tR = ve.last()
                b = bank()
                pe.wait(t_tok)
                for k in range(4):
                    tk = mm(b.ap[:, k * 64:k * 64 + 64],
                            [(Yk[:, k, :], vT[:, hf, k * P + lo:k * P + lo + 64])], signal=k == 3)
                b.free = [AC(XV, b.ap[:, 0:256].rearrange("p (q i) -> p q i", q=4), ACT.Copy, tk)]
                b = bank()
                pe.wait(ac.last(), tR)
                for k in range(4):
                    tk = mm(b.ap[:, k * 64:k * 64 + 64], [(R[:, k, :], XV[:, k, :])], signal=k == 3)
                b.free = [CP(U0[:, hf, par, :, :], b.ap[:, 0:256].rearrange("p (q i) -> p q i", q=4), tk)]
                b = bank()
                for k in range(4):
                    tk = mm(b4(b)[lo:lo + 64, k, :], [(alT[:, hf, k * P + lo:k * P + lo + 64], R[:, k, :])],
                            signal=k == 3)
                b.free = [CP(WT[lo:lo + 64, :, ts], b4(b)[lo:lo + 64, :, :], tk)]
            dump("ar", AR_[0])
            t_yv = ac.last()
            t_u0 = ve.add(lambda e: e.memset(ST[:, 0, :, :], 0.0))
            ELc = EL.rearrange("p k (c s) -> p k c s", s=32)
            t_s = t_u0
            tS = XV
            for c in range(8):
                hf, rb = c // 4, 32 * (c % 4)
                cs = slice(c * 32, c * 32 + 32)
                for par in range(2):
                    lo = 64 * par
                    b = bank()
                    pe.wait(t_s)
                    for k in range(4):
                        tk = mm(b.ap[rb:rb + 32, k * 64:k * 64 + 64], [(WT[lo:lo + 64, k, cs], ST[lo:lo + 64, c, k, :])],
                                signal=k == 3)
                    b.free = [TT(U[rb:rb + 32, hf, par, :, :],
                                 b.ap[rb:rb + 32, 0:256].rearrange("p (q i) -> p q i", q=4),
                                 U0[rb:rb + 32, hf, par, :, :], ALU.add, tk)]
                if c == 7:
                    break
                b = bank()
                pe.wait(ve.last())
                for k in range(4):
                    for par in range(2):
                        lo = 64 * par
                        f = slice(k * P + lo, k * P + lo + 64)
                        tk = mm(b.ap[lo:lo + 64, k * 64:k * 64 + 64],
                                [(kdT[rb:rb + 32, hf, f], vT[rb:rb + 32, hf, f]),
                                 (beT[rb:rb + 32, hf, f], U[rb:rb + 32, hf, par, k, :])],
                                signal=k == 3 and par == 1)
                b.free = [TT(tS, b.ap[:, 0:256].rearrange("p (q i) -> p q i", q=4), ST[:, c, :, :], ALU.add, tk)]
                t_s = TT(ST[:, c + 1, :, :], tS, ELc[:, :, c, 31:32].broadcast_to([P, 4, 64]), ALU.mult)
            t_u = ve.last()
            for g in range(4):
                hf, par = g // 2, g % 2
                lo, ts = 64 * par, slice(hf * P, hf * P + P)
                b = bank()
                pe.wait(t_u)
                for k in range(4):
                    o = b.ap[lo:lo + 64, k * P:(k + 1) * P]
                    f = slice(k * P + lo, k * P + lo + 64)
                    mm(o, [(U[:, hf, par, k, :], AR_[g][:, k, :])], stop=False, signal=False)
                    for c in range(4):
                        tk = mm(o[:, c * 32:c * 32 + 32],
                                [(ST[lo:lo + 64, 4 * hf + c, k, :], rd[lo:lo + 64, k, hf * P + c * 32:hf * P + c * 32 + 32])],
                                start=False, stop=c == 3, signal=k == 3 and c == 3)
                b.free = [TT(Yy[lo:lo + 64, :, ts], b4(b)[lo:lo + 64, :, :], Yy[lo:lo + 64, :, ts], ALU.add, tk, t_yv)]
            dump("y", Yy)
            M4, S4 = al, be
            proj("in_g", XN, ev_g)
            blksum(Yy, M4, 1.0 / 64, ve.last())
            t = TT(Yy, Yy, M4, ALU.subtract)
            t = AC(S4, Yy, ACT.Square, t)
            blksum(S4, M4, 1.0 / 64, t)
            TS(M4, M4, 64e-5, None, ALU.add, None)
            t = REC(M4, M4)
            t = AC(M4, M4, ACT.Sqrt, t)
            TT(Yy, Yy, M4, ALU.mult, t)
            for k in range(4):
                TS(Yy[:, k, :], Yy[:, k, :], vc("ln_g", k), vc("ln_b", k), ALU.mult, ALU.add)
            TT(Yy, Yy, BON, ALU.add)
            t_or = TT(Yy, Yy, Gg, ALU.mult)
            dump("orw", Yy)

            MIX = XN
            cm, cr = chunk("pm", 0), chunk("pr", 0)
            pe.wait(cm.tok, cr.tok, t_or, t_om)
            mA = Buf([kd[:, 2 * i:2 * i + 2, :] for i in range(2)])
            t_or = [t_or, ac.last()]
            for f in range(0, 8, 2):
                bs = []
                for c, src in ((cm, Om), (cr, Yy)):
                    b = bank()
                    for g in range(2):
                        tk = mm(b.ap[:, g * T:(g + 1) * T], [(c.ap[:, k, (f + g) * P:(f + g + 1) * P], src[:, k, :])
                                                             for k in range(4)], signal=g == 1)
                    c.done = tk
                    bs.append((b, tk))
                m = mA.next()
                v2 = [b.ap.rearrange("p (n t) -> p n t", n=2) for b, _ in bs]
                bs[0][0].free = [TT(m.ap, v2[0], Gt[:, f:f + 2, :], ALU.mult, bs[0][1], t_or)]
                bs[1][0].free = [TT(MIX[:, f:f + 2, :], v2[1], Gt[:, 8 + f:10 + f, :], ALU.mult, bs[1][1])]
                TT(MIX[:, f:f + 2, :], MIX[:, f:f + 2, :], m.ap, ALU.add)

            def ev_h(bv, f, n, tok):
                for g in range(n):
                    t = STT(X[:, f + g, :], bv[:, g, :], mod[:, 16 + f + g:17 + f + g], X[:, f + g, :],
                            ALU.mult, ALU.add, tok)
                return t

            proj("wo", MIX, ev_h, ve.last())
            dump("h", X)
            barrier()

            B = Arena(ar, 0, ARENA)
            G2 = B.take(64 * T)
            Bq = Arena(ar, 0, 64 * T)
            sq = Bq.tiles(8)
            rs = Bq.take(T)
            t = AC(sq, X, ACT.Square)
            b, t = colsum(sq, 8, t)
            t_r = rstd_of(rs, b.ap[:, 0:T], 1.0 / 1024, 1e-6, t)
            b.free = [ve.last()]
            TT(sq, X, bc(rs, 8), ALU.mult, t_r)
            STT(mod[:, 48:56], mod[:, 32:40], 1.0, vc("n2", 0, 8), ALU.add, ALU.mult)
            for k in range(8):
                t_xn = TS(XN[:, k, :], sq[:, k, :], mod[:, 48 + k:49 + k], mod[:, 24 + k:25 + k], ALU.mult, ALU.add)
            dump("xn2", XN)
            Qp = Bq.tiles(16)

            def ev_q(bv, f, n, tok):
                return AC(Qp[:, f:f + 2, :], bv, ACT.Copy, tok)

            proj("wq", XN, ev_q, t_xn)
            t_q = ac.last()
            sub = chunk("sub", 0)
            pe.wait(sub.tok, t_q)
            idT = B.take(3 * T).rearrange("p (a t) -> p a t", a=3)
            for tt in range(2):
                M = Arena(ar, 64 * T + 3 * T, ARENA)
                S = M.take(2048).rearrange("p (g n) -> p g n", g=16)
                for g in range(0, 16, 4):
                    b = bank()
                    for k in range(4):
                        tk = mm(b.ap[:, k * P:(k + 1) * P], [(Qp[:, g + k, tt * P:(tt + 1) * P],
                                                              sub.flat[:, (g + k) * P:(g + k + 1) * P])], signal=k == 3)
                    sub.done = tk
                    b.free = [AC(S[:, g:g + 4, :], b.ap.rearrange("p (q n) -> p q n", q=4), ACT.Copy, tk, ve.last())]
                t_S = ac.last()
                top = M.take(256).rearrange("p (g k) -> p g k", g=16)
                ti = M.take(256).bitcast(U32).rearrange("p (g k) -> p g k", g=16)
                tif = M.take(256).rearrange("p (h a k) -> p h a k", h=8, a=2)

                def top16(src, vals, idx, *w):
                    for r in range(2):
                        v8, i8 = vals[:, 8 * r:8 * r + 8], idx[:, 8 * r:8 * r + 8]
                        ve.add(lambda e, v8=v8: e.max(v8, src), *w)
                        ve.add(lambda e, v8=v8, i8=i8: e.max_index(i8, v8, src))
                        if r == 0:
                            ve.add(lambda e, v8=v8: e.match_replace(src, v8, src, -3.0e38))

                for g in range(16):
                    top16(S[:, g, :], top[:, g, :], ti[:, g, :], t_S)
                CP(tif.rearrange("p h a k -> p (h a k)"), ti.rearrange("p g k -> p (g k)"))
                tv = top.rearrange("p (h a) k -> p h a k", a=2)
                cand = M.take(2048).rearrange("p (h x) -> p h x", h=8)
                for h in range(8):
                    TT(cand[:, h, :].rearrange("p (a b) -> p a b", a=16),
                       tv[:, h, 0, :].unsqueeze(2).broadcast_to([P, 16, 16]),
                       tv[:, h, 1, :].unsqueeze(1).broadcast_to([P, 16, 16]), ALU.add)
                bs_ = M.take(128).rearrange("p (h k) -> p h k", h=8)
                bj = M.take(128).bitcast(U32).rearrange("p (h k) -> p h k", h=8)
                for h in range(8):
                    top16(cand[:, h, :], bs_[:, h, :], bj[:, h, :])
                g_ = M.take(128).rearrange("p (h k) -> p h k", h=8)
                TT(g_, bs_, bs_[:, :, 0:1].broadcast_to([P, 8, 16]), ALU.subtract)
                t = AC(g_, g_, ACT.Exp, ve.last())
                ve.add(lambda e: e.reduce_sum(small[:, 40:48], g_, AX.X), t)
                REC(small[:, 40:48], small[:, 40:48])
                TT(g_, g_, small[:, 40:48].unsqueeze(2).broadcast_to([P, 8, 16]), ALU.mult)
                bju = bj.rearrange("p h k -> p (h k)")
                fi = [M.take(128), M.take(128)]
                sel = [M.take(128), M.take(128)]
                raw = M.take(128).bitcast(U32)
                oh = cand.rearrange("p h x -> p (h x)")
                for a in range(2):
                    if a == 0:
                        ve.add(lambda e: e.tensor_single_scalar(raw, bju, 4, ALU.logical_shift_right))
                    else:
                        ve.add(lambda e: e.tensor_single_scalar(raw, bju, 15, ALU.bitwise_and))
                    CP(fi[a], raw)
                    o3 = oh.rearrange("p (x k) -> p x k", k=16)
                    TT(o3, fi[a].unsqueeze(2).broadcast_to([P, 128, 16]),
                       cst("iota", 0, 16).unsqueeze(1).broadcast_to([P, 128, 16]), ALU.is_equal)
                    for h in range(8):
                        o2 = oh[:, h * 256:(h + 1) * 256].rearrange("p (x k) -> p x k", k=16)
                        TT(o2, o2, tif[:, h, a, :].unsqueeze(1).broadcast_to([P, 16, 16]), ALU.mult)
                    ve.add(lambda e, a=a: e.reduce_sum(sel[a], o3, AX.X))
                b = bank()
                pe.wait(ve.last())
                for i, s in enumerate((sel[0], sel[1], g_.rearrange("p h k -> p (h k)"))):
                    tk = tr(b.ap[:, i * P:(i + 1) * P], s, signal=i == 2)
                b.free = [CP(idT[:, :, tt * P:(tt + 1) * P], b.ap[:, 0:384].rearrange("p (a t) -> p a t", a=3), tk)]
            dump("idT", idT)
            barrier()

            M = Arena(ar, 64 * T + 3 * T, ARENA)
            ohi = Buf([M.take(64) for _ in range(16)])
            ohj = Buf([M.take(128) for _ in range(16)])
            HA = Buf([M.take(512).rearrange("p (n t) -> p n t", n=2) for _ in range(3)])
            HG = Buf([M.take(512).rearrange("p (n t) -> p n t", n=2) for _ in range(3)])
            G3 = G2.rearrange("p (i t) -> p i t", i=64)
            acc = banks[4:8]
            pool_banks[0], pool_banks[1] = [0, 1, 2, 3], 0
            pe.wait(*[b.free for b in acc])
            prev_mul = None
            for half in range(2):
                for t0 in range(0, T, 8):
                    b = bank()
                    for j in range(8):
                        t = t0 + j
                        oi, oj = ohi.next(), ohj.next()
                        TS(oi.ap, cst("iota", 64 * half, 64 * half + 64), idT[:, 0, t:t + 1], idT[:, 2, t:t + 1],
                           ALU.is_equal, ALU.mult, oi.free)
                        tk = TS(oj.ap, cst("iota"), idT[:, 1, t:t + 1], None, ALU.is_equal, None, oj.free)
                        tk = mm(b.ap[:, j * 64:j * 64 + 64], [(oj.ap, oi.ap)], tk)
                        oi.free = oj.free = [tk]
                    b.free = [AC(G3[:, :, t0:t0 + 8].rearrange("p i t -> p t i"),
                                 b.ap.rearrange("p (t i) -> p t i", t=8), ACT.Copy, tk, prev_mul)]
                t_G = ac.last()
                pend = []

                def down(item):
                    hg, cv, q, first, last, rel = item
                    pe.wait(cv.tok, hg.tok)
                    for n in range(2):
                        ii = q * 2 + n
                        for tt in range(2):
                            for dh in range(2):
                                fst = first and n == 0
                                lst = last and n == 1
                                tk = mm(acc[tt * 2 + dh].ap, [(hg.ap[:, n, tt * P:(tt + 1) * P],
                                                               cv.ap[:, ii, dh * 512:dh * 512 + 512])],
                                        start=fst, stop=lst, signal=n == 1 and tt == 1 and dh == 1)
                    hg.free = [tk]
                    cv.done = tk

                for g in range(16):
                    cu = chunk("u", half * 16 + g)
                    cv = chunk("v", half * 16 + g)
                    for q in range(2):
                        b = bank()
                        bv = b.ap.rearrange("p (n t) -> p n t", n=2)
                        pe.wait(cu.tok)
                        for n in range(2):
                            f = q * 2 + n
                            tk = mm(bv[:, n, :], [(cu.ap[:, k, f * P:(f + 1) * P], XN[:, k, :]) for k in range(8)],
                                    signal=n == 1)
                        cu.done = tk
                        ha, hg = HA.next(), HG.next()
                        t = AC(ha.ap, bv, ACT.Gelu, tk, ha.free)
                        b.free = [t]
                        i0 = g * 4 + q * 2
                        hg.tok = TT(hg.ap, ha.ap, G3[:, i0:i0 + 2, :], ALU.mult, t, t_G, hg.free)
                        ha.free = [hg.tok]
                        prev_mul = hg.tok
                        pend.append((hg, cv, q, half == 0 and g == 0 and q == 0, half == 1 and g == 15 and q == 1, None))
                        if len(pend) > 1:
                            down(pend.pop(0))
                while pend:
                    down(pend.pop(0))
            t_acc = pe.last()
            ot = G2[:, 0:2048].rearrange("p (t d) -> p t d", t=2)
            for tt in range(2):
                for dh in range(2):
                    q = AC if dh else None
                    o = ot[:, tt, dh * 512:dh * 512 + 512]
                    src = acc[tt * 2 + dh]
                    if dh:
                        src.free = [AC(o, src.ap, ACT.Copy, t_acc, prev_mul)]
                    else:
                        src.free = [CP(o, src.ap, t_acc)]
            tw = [ve.last(), ac.last()]
            for k in range(0, 8, 2):
                b = bank()
                pe.wait(tw)
                for g in range(2):
                    for tt in range(2):
                        tk = tr(b.ap[:, g * T + tt * P:g * T + (tt + 1) * P], ot[:, tt, (k + g) * P:(k + g + 1) * P],
                                signal=g == 1 and tt == 1)
                for g in range(2):
                    b.free = [STT(X[:, k + g, :], b.ap[:, g * T:(g + 1) * T], mod[:, 40 + k + g:41 + k + g],
                                  X[:, k + g, :], ALU.mult, ALU.add, tk)]
            pool_banks[0], pool_banks[1] = list(range(8)), 0
            dump("h1", X)
            barrier()

            B = Arena(ar, 0, ARENA)
            K2 = B.take(C2W)
            ac.add(lambda e: e.dma_start(K2, D["con2"]).then_inc(s_ld2, 16), signal=False)
            LD2 = (s_ld2, 16)

            def c2(name):
                o, w = C2[name]
                return K2[:, o:o + w]

            keep = B.at
            QK = B.tiles(16)
            V2 = B.take(4096).rearrange("p (t f) -> p t f", t=2)
            Gs = B.tiles(16)
            tb = Buf([B.tiles(4) for _ in range(2)])

            def rope_pair(o, x1x2, cos, sin, tok):
                s = tb.next()
                TT(s.ap[:, 0:2, :], x1x2, bc(cos, 2), ALU.mult, tok, LD2)
                t = TT(s.ap[:, 2:4, :], x1x2, bc(sin, 2), ALU.mult)
                TT(o[:, 0, :], s.ap[:, 0, :], s.ap[:, 3, :], ALU.subtract)
                TT(o[:, 1, :], s.ap[:, 1, :], s.ap[:, 2, :], ALU.add)
                return t

            def ev_rope(bv, f, n, tok):
                return rope_pair(QK[:, f:f + 2, :], bv, c2("cosA"), c2("sinA"), tok)

            def ev_tok(dst):
                return lambda bv, tt, f, tok: AC(dst[:, tt, f:f + 512], bv, ACT.Copy, tok)

            sgb = Buf([B.tiles(2) for _ in range(2)])

            def ev_silu(dst):
                def consume(bv, f, n, tok):
                    s = sgb.next()
                    t = AC(s.ap, bv, ACT.Sigmoid, tok, s.free)
                    t = TT(dst[:, f:f + 2, :], bv, s.ap, ALU.mult, t)
                    s.free = [t]
                    return t
                return consume

            proj("a_qk", X, ev_rope, ve.last())
            proj_tok("a_v", X, ev_tok(V2))
            t_v = ac.last()
            proj("a_g", X, ev_silu(Gs))
            O2 = B.tiles(16)
            PTb = Buf([B.take(384) for _ in range(2)])
            t_qk = ve.last()
            for h in range(4):
                b = bank()
                pe.wait(t_qk, t_v)
                q, k = QK[:, 2 * h:2 * h + 2, :], QK[:, 8 + 2 * h:10 + 2 * h, :]
                mm(b.ap[:, 0:256], [(k[:, d, 0:128], q[:, d, :]) for d in range(2)], signal=False)
                tk = mm(b.ap[:, 256:384], [(k[:, d, 128:256], q[:, d, 128:256]) for d in range(2)])
                p = PTb.next()
                t = TT(p.ap, b.ap[:, 0:384], c2("dec")[:, h * 384:(h + 1) * 384], ALU.mult, tk, p.free)
                b.free = [t]
                for f in range(0, 4, 2):
                    b = bank()
                    pe.wait(t)
                    for g in range(2):
                        c = h * 512 + (f + g) * P
                        mm(b.ap[:, g * T:(g + 1) * T], [(V2[:, 0, c:c + P], p.ap[:, 0:256])], stop=False, signal=False)
                        tk = mm(b.ap[:, g * T + P:(g + 1) * T], [(V2[:, 1, c:c + P], p.ap[:, 256:384])], start=False,
                                signal=g == 1)
                    b.free = [AC(O2[:, 4 * h + f:4 * h + f + 2, :], b.ap.rearrange("p (n t) -> p n t", n=2),
                                 ACT.Copy, tk)]
                p.free = [tk]
            mean, rsd = B.take(T), B.take(T)

            def normalise(x, nk, eps, sqbuf, *w):
                b, t = colsum(x, nk, *w)
                b.free = [TS(mean, b.ap[:, 0:T], 1.0 / (nk * P), None, ALU.mult, None, t)]
                t = TT(x, x, bc(mean, nk), ALU.subtract)
                t = AC(sqbuf, x, ACT.Square, t)
                b, t = colsum(sqbuf, nk, t)
                t = rstd_of(rsd, b.ap[:, 0:T], 1.0 / (nk * P), eps, t)
                b.free = [ve.last()]
                return TT(x, x, bc(rsd, nk), ALU.mult, t)

            for h in range(4):
                normalise(O2[:, 4 * h:4 * h + 4, :], 4, 1e-5, QK[:, 0:4, :], ac.last(), ve.last())
            t = TT(O2, O2, Gs, ALU.mult)
            dump("o2", O2)
            alpha = float(4.0 ** 0.25)

            def ev_res(bv, f, n, tok):
                return STT(X[:, f:f + 2, :], X[:, f:f + 2, :], alpha, bv, ALU.mult, ALU.add, tok)

            def layer_norm(l, sqbuf):
                normalise(X, 8, 1e-5, sqbuf, ve.last())
                for k in range(8):
                    t = TS(X[:, k, :], X[:, k, :], vc("g2", 8 * l + k), vc("b2", 8 * l + k), ALU.mult, ALU.add)
                return t

            proj("a_o", O2, ev_res, t)
            t_x = layer_norm(0, QK[:, 0:8, :])
            dump("x1", X)
            barrier()

            B = Arena(ar, keep, ARENA)
            lat = B.tiles(4)
            kr = B.tiles(2)
            Kn = B.tiles(16)
            V3 = B.take(4096).rearrange("p (t f) -> p t f", t=2)
            Ql = B.tiles(6)
            Qr = B.tiles(8)
            mk = B.at
            sgb = Buf([B.tiles(2) for _ in range(2)])
            sq6 = B.tiles(6)
            rsd = B.take(T)
            mean = B.take(T)

            def ev_cp(dst):
                return lambda bv, f, n, tok: AC(dst[:, f:f + n, :], bv, ACT.Copy, tok)

            proj("kvd", X, ev_cp(lat), t_x)
            proj("kvr", X, ev_cp(kr))
            t_kr = ac.last()
            proj("b_q4", X, ev_cp(Ql))
            proj("b_q2", X, ev_cp(Ql[:, 4:6, :]))
            t_ql = ac.last()

            def rms(x, nk, gname, *w):
                t = AC(sq6[:, 0:nk, :], x, ACT.Square, ve.last(), pe.last(), *w)
                b, t = colsum(sq6, nk, t)
                t = rstd_of(rsd, b.ap[:, 0:T], 1.0 / (nk * P), 1e-6, t)
                b.free = [ve.last()]
                ve.wait(t)
                for k in range(nk):
                    t = STT(x[:, k, :], x[:, k, :], vc(gname, k), rsd, ALU.mult, ALU.mult)
                return t

            t_lat = rms(lat, 4, "kvn")
            t_qn = rms(Ql, 6, "bq")

            def rotB(x, n, o, tok):
                b = bank()
                bv = b.ap[:, 0:n * T].rearrange("p (n t) -> p n t", n=n)
                tk = mm(bv, [(cst("rotB"), x)], tok)
                s = sq6[:, 0:n, :]
                t = TT(s, bv, bc(c2("sinB"), n), ALU.mult, tk)
                b.free = [t]
                TT(o, x, bc(c2("cosB"), n), ALU.mult)
                return TT(o, o, s, ALU.add)

            rotB(kr[:, 0:1, :], 1, kr[:, 1:2, :], t_kr)
            proj("kvk", lat, ev_cp(Kn), t_lat)
            proj_tok("kvv", lat, ev_tok(V3))
            Qn = B.tiles(16)
            proj("uqn", Ql, ev_cp(Qn), t_qn)

            def ev_qr(bv, f, n, tok):
                return AC(Qr[:, f:f + 2, :], bv, ACT.Copy, tok)

            proj("uqr", Ql, ev_qr)
            t = ac.last()
            for f in range(0, 8, 2):
                t_rq = rotB(Qr[:, f:f + 2, :], 2, Qr[:, f:f + 2, :], t)
            t_kn = t
            dump("qr", Qr)
            O3 = Qn

            def evac3(h, b, tok):
                return AC(O3[:, h, :], b, ACT.Copy, tok)

            def parts3(h):
                lo = 64 * (h % 2)
                return [(Qn[:, h, :], Kn[:, h, :]), (Qr[lo:lo + 64, h // 2, :], kr[lo:lo + 64, 1, :])]

            attention(B, 16, 128, float(192.0 ** -0.5), parts3, lambda h, kt: V3[:, kt, h * P:(h + 1) * P],
                      lambda h: 0, evac3, t_rq, t_kn)
            t_o = ac.last()
            dump("o3", O3)
            Gs = Kn
            pe.wait(t_o)
            ac.wait(pe.last())
            ve.wait(pe.last(), t_o)

            def ev_gate(bv, f, n, tok):
                s = sgb.next()
                t = AC(s.ap, bv, ACT.Sigmoid, tok, s.free)
                t = TT(s.ap, bv, s.ap, ALU.mult, t)
                s.free = [TT(O3[:, f:f + 2, :], O3[:, f:f + 2, :], s.ap, ALU.mult)]
                return t

            proj("b_g", X, ev_gate)
            proj("b_o", O3, ev_res, ve.last())
            layer_norm(1, V3.rearrange("p t f -> p (t f)")[:, 0:2048].rearrange("p (k t) -> p k t", k=8))
            dump("xf", X)

        try:
            stages()
        except Stop:
            pass
        fin = [q.last() for q in (pe, ve, ac, po) if q.n]
        sp_out = fin

        for c in chunks:
            if c.idx >= NSLOT:
                sp.wait(chunks[c.idx - NSLOT].done)
            sp.add(lambda e, c=c: e.dma_start(c.flat, D[c.name][c.j]).then_inc(slot_sem[c.idx % NSLOT], 16), signal=False)
        sp.wait(LDX, LD, *sp_out)
        sp.add(lambda e: e.dma_start(out, Xt[:, :]).then_inc(s_out, 16), signal=False)
        sp.wait((s_out, 16))

        block = ctx.enter_context(nc.Block())

        @block.sync
        def _(e):
            sp.run(e)

        @block.scalar
        def _(e):
            ac.run(e)

        @block.vector
        def _(e):
            ve.run(e)

        @block.gpsimd
        def _(e):
            po.run(e)

        @block.tensor
        def _(e):
            pe.run(e)


def constants():
    a = np.zeros((P, C1W), np.float32)

    def put(name, v):
        o, w = C1[name]
        a[:, o:o + w] = v

    r = np.arange(P)
    row, col = r[:, None], r[None, :]
    put("ident", np.eye(P))
    put("ones", 1.0)
    put("blk", row // 64 == col // 64)
    rot = np.zeros((P, P))
    for h in range(2):
        for d in range(8):
            rot[64 * h + d + 8, 64 * h + d] = -1
            rot[64 * h + d, 64 * h + d + 8] = 1
    put("rotA", rot)
    rot = np.zeros((P, P))
    for h in range(2):
        for d in range(32):
            rot[64 * h + d + 32, 64 * h + d] = -1
            rot[64 * h + d, 64 * h + d + 32] = 1
    put("rotB", rot)
    put("mXd", (row // 16 == col // 16) & (col < row))
    put("mXo", (row // 32 == col // 32) & (row // 16 != col // 16) & (col < row))
    put("mYd", (row // 16 == col // 16) & (row < col))
    put("m32s", (row // 32 == col // 32) & (row < col))
    put("m32i", (row // 32 == col // 32) & (row <= col))
    tri = np.where(col <= row, 0.0, NEG)
    put("mask3", np.concatenate([tri, np.zeros((P, P)), tri], 1))
    put("reset", (np.arange(256) % 32 != 0)[None, :] * np.ones((P, 1)))
    put("iota", col * np.ones((P, 1)))
    inv = np.zeros(P, np.float32)
    e = np.float32(500000.0) ** (-(np.arange(8, dtype=np.float32) * np.float32(2.0)) / np.float32(16))
    for h in range(2):
        for s in range(2):
            inv[64 * h + 8 * s:64 * h + 8 * s + 8] = e
    put("inv", inv[:, None])
    b = np.zeros((P, C2W), np.float32)

    def put2(name, v):
        o, w = C2[name]
        b[:, o:o + w] = v

    t = np.arange(T, dtype=np.float32)
    f = np.float32(10000.0) ** (-np.arange(128, dtype=np.float32) / np.float32(128))
    ang = (f[:, None] * t[None, :]).astype(np.float32)
    put2("cosA", np.cos(ang.astype(np.float64)))
    put2("sinA", np.sin(ang.astype(np.float64)))
    f = np.float32(10000.0) ** (-np.arange(32, dtype=np.float32) / np.float32(32))
    ang = np.tile((f[:, None] * t[None, :]).astype(np.float32), (4, 1))
    put2("cosB", np.cos(ang.astype(np.float64)))
    put2("sinB", np.sin(ang.astype(np.float64)))
    dec = []
    for h in range(4):
        lg = np.log1p(-2.0 ** (-5.0 - h))
        d = np.arange(T)[None, :] - r[:, None]
        m = np.where(d >= 0, np.exp(np.maximum(d, 0) * lg), 0.0) / 16.0
        dec += [m, m[:, 0:128]]
    put2("dec", np.concatenate(dec, 1))
    return a, b


def lay_weights(i):
    def tile(w, nf):
        k, f = w.shape
        kt, nch = k // P, f // (nf * P)
        return np.ascontiguousarray(w.reshape(kt, P, nch, nf * P).transpose(2, 1, 0, 3)).reshape(nch, P, kt * nf * P)

    def cols(w, *idx):
        return np.concatenate([w[:, a:b] for a, b in idx], 1)

    win = i["w_in"][0]
    z0 = 1536
    W = {}
    W["ada"] = tile(i["w_ada"][0], 4)
    W["in_wag"] = tile(win[:, z0 + 1536:z0 + 1792], 2)
    W["in_rkv"] = tile(win[:, z0:z0 + 1536], 4)
    W["in_v"] = tile(win[:, 1024:1536], 4)
    W["in_qk"] = tile(win[:, 0:1024], 4)
    W["in_g"] = tile(win[:, 3328:5376], 4)
    W["pm"] = tile(i["w_proj_moba"][0], 8)
    W["pr"] = tile(i["w_proj_rwkv"][0], 8)
    W["wo"] = tile(i["w_out"][0], 4)
    W["wq"] = tile(i["peer_wq"][0], 4)
    W["sub"] = np.ascontiguousarray(i["peer_subkeys"][0].transpose(3, 0, 1, 2)).reshape(1, P, 2048)
    W["u"] = tile(i["peer_u"][0].T, 4)
    W["v"] = np.ascontiguousarray(i["peer_v"][0].reshape(32, 4, P, 1024).transpose(0, 2, 1, 3)).reshape(32, P, 4096)
    a = i["a_w_in_2"][0]
    W["a_qk"] = tile(a[:, 0:2048], 4)
    W["a_v"] = tile(a[:, 2048:4096], 4)
    W["a_g"] = tile(a[:, 4096:6144], 4)
    W["a_o"] = tile(i["a_w_out_2"][0], 2)
    d = i["kv_w_down_2"]
    W["kvd"] = tile(d[:, 0:512], 4)
    W["kvr"] = tile(cols(d, (512, 576), (512, 576)), 1)
    up = i["kv_w_up_2"].reshape(512, 16, 256)
    W["kvk"] = tile(up[:, :, 0:128].reshape(512, 2048), 8)
    W["kvv"] = tile(up[:, :, 128:256].reshape(512, 2048), 8)
    b = i["b_w_in_2"][0]
    W["b_q4"] = tile(b[:, 0:512], 4)
    W["b_q2"] = tile(b[:, 512:768], 2)
    W["b_g"] = tile(b[:, 768:2816], 4)
    uq = i["b_w_uq_2"][0].reshape(768, 16, 192)
    W["uqn"] = tile(uq[:, :, 0:128].reshape(768, 2048), 4)
    W["uqr"] = tile(uq[:, :, 128:192].reshape(768, 1024), 4)
    W["b_o"] = tile(i["b_w_out_2"][0], 2)
    for n, w in W.items():
        kt, nf, nch = WEIGHTS[n]
        assert w.shape == (nch, P, kt * nf * P), (n, w.shape)
    return W


def lay_vectors(i):
    def v(x, n):
        return np.asarray(x).reshape(n, P).T

    mu = i["rwkv_mu"][0]
    mus = np.concatenate([mu[1536:1792], mu[0:1536]])
    parts = {
        "c": v(i["c"][0], 8), "b_ada": v(i["b_ada"][0], 48), "n1": v(i["norm1_g"][0], 8), "n2": v(i["norm2_g"][0], 8),
        "qg": np.tile(i["q_norm_g"][0], 2)[:, None], "kg": np.tile(i["k_norm_g"][0], 2)[:, None],
        "mu": v(mus, 14), "w0": v(i["rwkv_w0"][0], 4), "a0": v(i["rwkv_a0"][0], 4), "k_k": v(i["rwkv_k_k"][0], 4),
        "k_a": v(i["rwkv_k_a"][0], 4), "r_k": v(i["rwkv_r_k"][0].reshape(512), 4), "ln_g": v(i["rwkv_ln_g"][0], 4),
        "ln_b": v(i["rwkv_ln_b"][0], 4), "bq": v(i["b_q_norm_2"][0], 6), "kvn": v(i["kv_norm_2"], 4),
        "g2": v(i["ln_g_2"].reshape(2048), 16), "b2": v(i["ln_b_2"].reshape(2048), 16),
    }
    return np.ascontiguousarray(np.concatenate([parts[n] for n in VEC], 1))


def lay_inputs(inputs):
    i = {k: np.asarray(v) for k, v in inputs.items()}
    m = lay_weights(i)
    m["xT"] = np.ascontiguousarray(i["x"][0].T.reshape(8, P, T).transpose(1, 0, 2)).reshape(P, 8 * T)
    m["vec"] = lay_vectors(i)
    m["con"], m["con2"] = constants()
    m["w2a2"] = np.concatenate([i["rwkv_w2"][0], i["rwkv_a2"][0]], 0)
    m["g2"] = i["rwkv_g2"][0]
    m["pos"] = np.ascontiguousarray(np.broadcast_to(i["positions"], (P, T)))
    return {k: np.ascontiguousarray(v) for k, v in m.items()}


def kernel(**inputs):
    import concourse.bacc as _bacc
    from concourse.bass_utils import run_bass_kernel_spmd as _run

    nc = _bacc.Bacc("TRN2", target_bir_lowering=False, num_devices=1)
    arrays = {f"in_{k}": v for k, v in lay_inputs(inputs).items()}
    D = {k[3:]: nc.dram_tensor(k, list(v.shape), mybir.dt.from_np(v.dtype), kind="ExternalInput").ap()
         for k, v in arrays.items()}
    out = nc.dram_tensor("out_0", [P, 8 * T], F32, kind="ExternalOutput").ap()
    build_program(nc, D, out)
    r = _run(nc, [arrays], core_ids=[0])
    y = np.asarray(r.results[0]["out_0"])
    return np.ascontiguousarray(y.reshape(P, 8, T).transpose(2, 1, 0)).reshape(1, T, 1024)
```

```python
import concourse.bass as bass
from concourse import mybir
from concourse.alu_op_type import AluOpType as ALU
from contextlib import ExitStack, contextmanager
import numpy as np

F32 = mybir.dt.float32
F32R = mybir.dt.float32r
I32 = mybir.dt.int32
U32 = mybir.dt.uint32
ACT = mybir.ActivationFunctionType
AX = mybir.AxisListType
P = 128
T = 256
NEG = -1e30
PI = float(np.pi)

C1 = {}
_o = 0
for _n, _w in (("ident", 128), ("ones", 128), ("blk", 128), ("rotA", 128), ("rotB", 128), ("mXd", 128),
               ("mXo", 128), ("mYd", 128), ("m32s", 128), ("m32i", 128), ("mask3", 384), ("reset", 256),
               ("iota", 128), ("inv", 1), ("pad", 3)):
    C1[_n] = (_o, _w)
    _o += _w
C1W = _o
C2 = {"cosA": (0, 256), "sinA": (256, 256), "cosB": (512, 256), "sinB": (768, 256), "dec": (1024, 1536)}
C2W = 2560
VEC = {}
_o = 0
for _n, _w in (("c", 8), ("b_ada", 48), ("n1", 8), ("n2", 8), ("qg", 1), ("kg", 1), ("mu", 14), ("w0", 4),
               ("a0", 4), ("k_k", 4), ("k_a", 4), ("r_k", 4), ("ln_g", 4), ("ln_b", 4), ("bq", 6), ("kvn", 4),
               ("g2", 16), ("b2", 16)):
    VEC[_n] = (_o, _w)
    _o += _w
VECW = _o

WEIGHTS = {
    "ada": (8, 4, 12), "in_wag": (8, 2, 1), "in_rkv": (8, 4, 3), "in_v": (8, 4, 1), "in_qk": (8, 4, 2),
    "in_g": (8, 4, 4), "pm": (4, 8, 1), "pr": (4, 8, 1), "wo": (8, 4, 2), "wq": (8, 4, 4), "sub": (1, 16, 1),
    "u": (8, 4, 32), "v": (4, 8, 32),
    "a_qk": (8, 4, 4), "a_v": (8, 4, 4), "a_g": (8, 4, 4), "a_o": (16, 2, 4),
    "kvd": (8, 4, 1), "kvr": (8, 1, 1), "kvk": (4, 8, 2), "kvv": (4, 8, 2),
    "b_q4": (8, 4, 1), "b_q2": (8, 2, 1), "b_g": (8, 4, 4), "uqn": (6, 4, 4), "uqr": (6, 4, 2), "b_o": (16, 2, 4),
}
RAW = ("ada", "sub")
NSLOT = 3
SLOT = 4096
PIECE = 2048
NS = 2
BASE = NSLOT * SLOT
ARENA = BASE + 20100


def pieces(name):
    kt, nf, _ = WEIGHTS[name]
    return -(-kt * nf * P // PIECE)


class Queue:

    def __init__(self, sem, chained):
        self.sem, self.chained = sem, chained
        self.n = 0
        self.items = []
        self.met = {}

    def wait(self, *toks):
        for t in toks:
            if t is None:
                continue
            if isinstance(t, list):
                self.wait(*t)
                continue
            sem, v = t
            if v > self.met.get(id(sem), 0):
                self.met[id(sem)] = v
                self.items.append((None, sem, v))

    def add(self, fn, *toks, signal=True):
        if self.chained and self.n:
            self.wait((self.sem, self.n))
        self.wait(*toks)
        if not signal:
            self.items.append((fn, None, 0))
            return None
        self.n += 1
        self.items.append((fn, self.sem, 1))
        return (self.sem, self.n)

    def last(self):
        return (self.sem, self.n)

    @contextmanager
    def apart(self, *toks):
        self.wait(*toks)
        was, self.chained = self.chained, False
        yield
        self.chained = was

    def run(self, eng):
        for fn, sem, v in self.items:
            if fn is None:
                eng.wait_ge(sem, v)
            elif sem is None:
                fn(eng)
            else:
                fn(eng).then_inc(sem, v)


class Bank:

    def __init__(self, ap):
        self.ap = ap
        self.free = []


class Buf:

    def __init__(self, aps):
        self.slots = [Bank(a) for a in aps]
        self.i = -1

    def next(self):
        self.i = (self.i + 1) % len(self.slots)
        return self.slots[self.i]


class Arena:
    def __init__(self, t, lo, hi):
        self.t, self.at, self.hi = t, lo, hi

    def take(self, n):
        o = self.at
        self.at += n
        assert self.at <= self.hi, (self.at, self.hi)
        return self.t[:, o:o + n]

    def tiles(self, k, n=T):
        return self.take(k * n).rearrange("p (k t) -> p k t", k=k)


def build_program(nc, D, out, stop=None, dumps=None):
    with ExitStack() as ctx:
        hw = place(nc, ctx)
        order = queue_program(nc, ctx, D, out, hw, None, stop, dumps)
        queue_program(nc, ctx, D, out, hw, order, stop, dumps)


def place(nc, ctx):
    def sbuf(name, shape, dt=F32):
        return ctx.enter_context(nc.sbuf_tensor(name, shape, dt))

    hw = {
        "ar": sbuf("ar", [P, ARENA]), "con": sbuf("con", [P, C1W]), "vec": sbuf("vec", [P, VECW]),
        "mod": sbuf("mod", [P, 64]), "small": sbuf("small", [P, 96]), "X": sbuf("X", [P, 8 * T]),
        "RH": sbuf("RH", [P, 16 * T], F32R), "RL": sbuf("RL", [P, 16 * T], F32R),
        "WH": sbuf("WH", [P, NS * PIECE], F32R), "WL": sbuf("WL", [P, NS * PIECE], F32R),
        "ps": [ctx.enter_context(nc.psum_tensor(f"ps{i}", [P, 512], F32)) for i in range(8)],
    }
    for n in ["s_pe", "s_ve", "s_ac", "s_po", "s_sp", "s_ld", "s_ldx", "s_ld2", "s_out"] + [f"s_w{i}" for i in range(NSLOT)]:
        hw[n] = ctx.enter_context(nc.semaphore(n))
    return hw


def queue_program(nc, ctx, D, out, hw, order, stop=None, dumps=None):
    dry = order is None
    if True:
        def sem(name):
            return ctx.enter_context(nc.semaphore(name))

        ar, con, vec, mod, small, Xt = (hw[n] for n in ("ar", "con", "vec", "mod", "small", "X"))
        X = Xt[:, :].rearrange("p (k t) -> p k t", k=8)
        RH = hw["RH"][:, :].rearrange("p (k t) -> p k t", k=16)
        RL = hw["RL"][:, :].rearrange("p (k t) -> p k t", k=16)
        WH, WL = hw["WH"], hw["WL"]
        banks = [Bank(p[:, :]) for p in hw["ps"]]

        pe = Queue(hw["s_pe"], False)
        ve = Queue(hw["s_ve"], True)
        ac = Queue(hw["s_ac"], True)
        po = Queue(hw["s_po"], True)
        sp = Queue(hw["s_sp"], False)
        slot_sem = [hw[f"s_w{i}"] for i in range(NSLOT)]
        s_ld, s_ldx, s_ld2, s_out = (hw[n] for n in ("s_ld", "s_ldx", "s_ld2", "s_out"))

        def cst(name, lo=0, hi=None):
            o, w = C1[name]
            return con[:, o + lo:o + (w if hi is None else hi)]

        def vc(name, i=0, n=1):
            o, _ = VEC[name]
            return vec[:, o + i:o + i + n]

        ident, ones, blk = cst("ident"), cst("ones"), cst("blk")

        def TT(o, a, b, op, *w, q=ve):
            return q.add(lambda e: e.tensor_tensor(o, a, b, op), *w)

        def TS(o, a, s1, s2, op0, op1, *w, q=ve):
            if s2 is None:
                return q.add(lambda e: e.tensor_scalar(o, a, s1, None, op0), *w)
            return q.add(lambda e: e.tensor_scalar(o, a, s1, s2, op0, op1), *w)

        def STT(o, a, s, b, op0, op1, *w):
            return ve.add(lambda e: e.scalar_tensor_tensor(o, a, s, b, op0, op1), *w)

        def CP(o, a, *w, q=ve):
            return q.add(lambda e: e.tensor_copy(o, a), *w)

        def AC(o, a, f, *w, **k):
            return ac.add(lambda e: e.activation(o, a, f, **k), *w)

        def ACi(o, a, f, *w, **k):
            with ac.apart():
                return AC(o, a, f, *w, **k)

        def REC(o, a, *w):
            return ve.add(lambda e: e.reciprocal(o, a), *w)

        pool_banks = [list(range(7)), 0]

        def bank():
            ids, i = pool_banks
            pool_banks[1] = (i + 1) % len(ids)
            b = banks[ids[i % len(ids)]]
            pe.wait(b.free)
            b.free = []
            return b

        def mm(o, pairs, *w, start=True, stop=True, signal=True, skip=False):
            pe.wait(*w)
            tok = None
            for i, (l, r) in enumerate(pairs):
                last = i == len(pairs) - 1
                tok = pe.add(lambda e, l=l, r=r, s=(start and i == 0), t=(stop and last):
                             e.matmul(o, l, r, start=s, stop=t, skip_group_check=skip),
                             signal=signal and last)
            return tok

        def tr(o, a, signal=True):
            return pe.add(lambda e: e.transpose(o, a, ident), signal=signal)

        class Chunk:
            pass

        class Item:
            pass

        chunks, items = [], []
        slots = {"use": [0, 1], "at": 0, "last": [None] * NSLOT, "n": [0] * NSLOT, "extra": [[] for _ in range(NSLOT)]}
        lo_on = [ve]

        def load_chunk(name, j):
            kt, nf, _ = WEIGHTS[name]
            c = Chunk()
            c.name, c.j = name, j
            c.slot = s = slots["use"][slots["at"] % len(slots["use"])]
            slots["at"] += 1
            slots["n"][s] += 1
            c.tok = (slot_sem[s], 16 * slots["n"][s])
            c.before, slots["last"][s] = slots["last"][s], c
            c.wait, slots["extra"][s] = slots["extra"][s], []
            c.flat = ar[:, s * SLOT:s * SLOT + kt * nf * P]
            c.ap = c.flat.rearrange("p (k f) -> p k f", k=kt)
            c.free = []
            chunks.append(c)
            return c

        st_ = {"issued": 0, "taken": 0, "ni": 0, "nt": 0, "chunk": None}
        split_items = []

        def issue(key):
            name, j, pi = key
            it = Item()
            kt, nf, _ = WEIGHTS[name]
            if pi == 0:
                st_["chunk"] = load_chunk(name, j)
            c = it.chunk = st_["chunk"]
            it.done = None
            if name in RAW:
                it.tok = c.tok
                it.flat, it.ap = c.flat, c.ap
            else:
                n = pieces(name)
                fw = nf * P // n
                s = st_["ni"] % NS
                if name == "v":
                    src = c.flat[:, pi * PIECE:(pi + 1) * PIECE].rearrange("p (k f) -> p k f", k=2)
                    kt, fw = 2, 1024
                else:
                    src = c.ap[:, :, pi * fw:(pi + 1) * fw]
                h = WH[:, s * PIECE:s * PIECE + kt * fw].rearrange("p (k f) -> p k f", k=kt)
                l = WL[:, s * PIECE:s * PIECE + kt * fw].rearrange("p (k f) -> p k f", k=kt)
                before = split_items[st_["ni"] - NS].done if st_["ni"] >= NS else None
                m = max(kt // 2, 1)
                for a, z in ((0, m), (m, kt)) if kt > 1 else ((0, 1),):
                    h_, l_, s_ = h[:, a:z, :], l[:, a:z, :], src[:, a:z, :]
                    with ac.apart():
                        t = ac.add(lambda e, h_=h_, s_=s_: e.activation(h_, s_, ACT.Copy), c.tok, before)
                    with lo_on[0].apart():
                        t = lo_on[0].add(lambda e, h_=h_, l_=l_, s_=s_:
                                         e.tensor_tensor(l_, s_, h_.bitcast(F32), ALU.subtract), t, c.tok, before)
                it.tok, it.h, it.l = t, h, l
                c.free.append(t)
                st_["ni"] += 1
                split_items.append(it)
            items.append(it)

        def take(name, j, pi=0):
            key = (name, j, pi)
            if dry:
                items_order.append(key)
                issue(key)
                it = items[-1]
            else:
                assert order[st_["taken"]] == key, (order[st_["taken"]], key)
                while st_["issued"] < len(order):
                    k = order[st_["issued"]]
                    if k[0] in RAW:
                        if st_["issued"] - st_["taken"] > NS:
                            break
                    elif st_["issued"] > st_["taken"] and order[st_["issued"] - 1][0] in RAW:
                        break
                    elif st_["ni"] - st_["nt"] >= NS:
                        break
                    issue(k)
                    st_["issued"] += 1
                it = items[st_["taken"]]
            st_["taken"] += 1
            if name not in RAW:
                st_["nt"] += 1
            return it

        items_order = []

        def mm3(o, trip, *w, start=True, stop=True, signal=True):
            pairs = []
            for lh, ll, rh, rl in trip:
                pairs += [(lh, rh), (lh, rl), (ll, rh)]
            return mm(o, pairs, *w, start=start, stop=stop, signal=signal)

        def proj_steps(name, xs, consume, *w):
            kt, nf, nch = WEIGHTS[name]
            xh, xl = xs
            for j in range(nch):
                for pi in range(pieces(name)):
                    it = take(name, j, pi)
                    pe.wait(it.tok, *w)
                    nt = nf // pieces(name)
                    for f in range(0, nt, 2):
                        n = min(2, nt - f)
                        b = bank()
                        bv = b.ap[:, 0:n * T].rearrange("p (n t) -> p n t", n=n)
                        for g in range(n):
                            fs = slice((f + g) * P, (f + g + 1) * P)
                            tok = mm3(bv[:, g, :], [(it.h[:, k, fs], it.l[:, k, fs], xh[:, k, :], xl[:, k, :])
                                                    for k in range(kt)], signal=g == n - 1)
                        it.done = tok
                        b.free = [consume(bv, j * nf + pi * nt + f, n, tok)]
                    yield

        def proj(name, xs, consume, *w):
            for _ in proj_steps(name, xs, consume, *w):
                pass

        def proj_tok(name, xs, consume, *w):
            kt, nf, nch = WEIGHTS[name]
            xh, xl = xs
            fw = nf * P // pieces(name)
            for j in range(nch):
                for pi in range(pieces(name)):
                    it = take(name, j, pi)
                    pe.wait(it.tok, *w)
                    for tt in range(2):
                        ts = slice(tt * P, (tt + 1) * P)
                        b = bank()
                        tok = mm3(b.ap[:, 0:fw], [(xh[:, k, ts], xl[:, k, ts], it.h[:, k, :], it.l[:, k, :])
                                                  for k in range(kt)])
                        it.done = tok
                        b.free = [consume(b.ap[:, 0:fw], tt, j * nf * P + pi * fw, fw, tok)]

        def split_act(src, k0, *w):
            nk = src.shape[1]
            w = list(w) + [pe.last() if pe.n else None]
            for a in range(0, nk, 4):
                b = min(a + 4, nk)
                h, l = RH[:, k0 + a:k0 + b, :], RL[:, k0 + a:k0 + b, :]
                t = ACi(h, src[:, a:b, :], ACT.Copy, *w)
                with ve.apart():
                    t = TT(l, src[:, a:b, :], h.bitcast(F32), ALU.subtract, t, *w)
            return (RH[:, k0:k0 + nk, :], RL[:, k0:k0 + nk, :]), t

        def barrier():
            toks = [q.last() for q in (pe, ve, ac, po) if q.n]
            for q in (pe, ve, ac, po):
                q.wait(toks)

        class Stop(Exception):
            pass

        def dump(name, ap):
            if dumps is not None and name in dumps:
                barrier()
                toks = [q.last() for q in (pe, ve, ac, po) if q.n]
                po.wait(toks)
                s = hw.setdefault("s_d_" + name, None) or sem("s_d_" + name)
                hw["s_d_" + name] = s
                po.add(lambda e: e.dma_start(dumps[name], ap).then_inc(s, 16), signal=False)
                po.wait((s, 16))
            if stop == name:
                raise Stop

        def rstd_of(o, src, scale, eps, *w):
            TS(o, src, scale, eps, ALU.mult, ALU.add, *w)
            t = REC(o, o)
            return AC(o, o, ACT.Sqrt, t)

        def colsum(x, nk, *w):
            b = bank()
            return b, mm(b.ap[:, 0:T], [(ones, x[:, k, :]) for k in range(nk)], *w)

        def bc(ap, n):
            return ap.unsqueeze(1).broadcast_to([P, n, T])

        ac.add(lambda e: e.dma_start(Xt[:, :], D["xT"]).then_inc(s_ldx, 16), signal=False)
        ac.add(lambda e: e.dma_start(vec[:, :], D["vec"]).then_inc(s_ldx, 16), signal=False)
        ac.add(lambda e: e.dma_start(con[:, :], D["con"]).then_inc(s_ldx, 16), signal=False)
        LDX = (s_ldx, 48)
        A = Arena(ar, 2 * SLOT, ARENA)
        lw = A.take(1024)
        posi = A.take(T)
        ac.add(lambda e: e.dma_start(lw[:, 0:512], D["w2a2"]).then_inc(s_ld, 16), signal=False)
        ac.add(lambda e: e.dma_start(lw[:, 512:1024], D["g2"]).then_inc(s_ld, 16), signal=False)
        ac.add(lambda e: e.dma_start(posi.bitcast(I32), D["pos"]).then_inc(s_ld, 16), signal=False)
        LD = (s_ld, 48)

        def stages():
            asum = Buf([A.take(512) for _ in range(2)])

            def ada_steps(j0, j1, parts, lag, *w):
                b = banks[7]
                pe.wait(b.free)
                due = []

                def add_up():
                    nonlocal tok
                    j, s, ts = due.pop(0)
                    for f in range(4):
                        tok = mm(b.ap[:, 4 * j + f:4 * j + f + 1],
                                 [(s.ap[:, f * P:(f + 1) * P], cst("ones", 0, 1))], ts, signal=f == 3)
                    s.free = [tok]

                tok = None
                for j in range(j0, j1):
                    it = take("ada", j)
                    s = asum.next()
                    ts = []
                    for q, lo, hi in parts:
                        o = s.ap[:, lo:hi]
                        if q is po:
                            v = it.ap[:, :, lo:hi]
                            TT(v, v, small[:, 0:8].unsqueeze(2).broadcast_to([P, 8, hi - lo]), ALU.mult,
                               it.tok, s.free, list(w), q=q)
                            TT(v[:, 0:4, :], v[:, 0:4, :], v[:, 4:8, :], ALU.add, q=q)
                            TT(v[:, 0:2, :], v[:, 0:2, :], v[:, 2:4, :], ALU.add, q=q)
                            ts.append(TT(o, v[:, 0, :], v[:, 1, :], ALU.add, q=q))
                            continue
                        t = TS(o, it.ap[:, 0, lo:hi], small[:, 0:1], None, ALU.mult, None, it.tok, s.free, list(w), q=q)
                        for k in range(1, 8):
                            with q.apart(t):
                                t = q.add(lambda e, o=o, a=it.ap[:, k, lo:hi], k=k: e.scalar_tensor_tensor(
                                    o, a, small[:, k:k + 1], o, ALU.mult, ALU.add))
                        ts.append(t)
                    it.chunk.free = ts
                    due.append((j, s, ts))
                    if len(due) > lag:
                        add_up()
                    yield
                while due:
                    add_up()
                lo, hi = 4 * j0, 4 * j1
                t = TT(mod[:, lo:hi], b.ap[:, lo:hi], vc("b_ada", lo, hi - lo), ALU.add, tok)
                b.free = [t]

            Aa, LDc = A.tiles(4), A.tiles(4)
            sq = ar[:, A.at - 2048:A.at].rearrange("p (k t) -> p k t", k=8)
            XN = sq
            rs = A.take(T)
            t = AC(small[:, 8:16], vc("c", 0, 8), ACT.Sigmoid, LDX)
            t_c = TT(small[:, 0:8], vc("c", 0, 8), small[:, 8:16], ALU.mult, t, LDX)
            t = AC(sq, X, ACT.Square)
            b, t = colsum(sq, 8, t)
            t_r = rstd_of(rs, b.ap[:, 0:T], 1.0 / 1024, 1e-6, t)
            b.free = [ve.last()]
            TT(sq, X, bc(rs, 8), ALU.mult, t_r)
            for _ in ada_steps(0, 4, ((ve, 0, 384), (po, 384, 512)), 0, t_c):
                pass
            STT(mod[:, 48:56], mod[:, 8:16], 1.0, vc("n1", 0, 8), ALU.add, ALU.mult)
            with ve.apart(ve.last()):
                for k in range(8):
                    t_xn = TS(XN[:, k, :], sq[:, k, :], mod[:, 48 + k:49 + k], mod[:, k:k + 1], ALU.mult, ALU.add)
            xs, t_xn = split_act(XN, 0, t_xn)
            dump("xn", XN)

            cA, sA, tmpr = A.take(T), A.take(T), posi
            CP(cA, posi.bitcast(I32), LD)
            TS(cA, cA, cst("inv"), None, ALU.mult, None)
            TS(tmpr, cA, float(1 / (2 * np.pi)), 12582912.0, ALU.mult, ALU.add)
            TS(tmpr, tmpr, 12582912.0, None, ALU.subtract, None)
            c1 = 6.28125
            c2 = float(np.float32(2 * np.pi - c1))
            c3 = float(2 * np.pi - c1 - c2)
            for cc in (c1, c2, c3):
                STT(cA, tmpr, -cc, cA, ALU.mult, ALU.add)
            t = TS(cA, cA, PI, -PI, ALU.min, ALU.max)
            t = AC(sA, cA, ACT.Sin, t)
            t = AC(cA, cA, ACT.Abs)
            t = TS(cA, cA, -1.0, PI / 2, ALU.mult, ALU.add, t)
            t_rope = AC(cA, cA, ACT.Sin, t)

            z_at = A.at
            Z = A.tiles(14)
            ztr = Buf([A.take(2 * 257).rearrange("p (n t) -> p n t", n=2) for _ in range(2)])
            Gt = ar[:, z_at:z_at + 4096].rearrange("p (k t) -> p k t", k=16)
            assert A.at - z_at >= 4096
            zd = A.tiles(2)
            att = Arena(ar, A.at - 1540, A.at + 384)
            A.take(384)
            for s in ztr.slots:
                s.free = [ve.add(lambda e, s=s: e.memset(s.ap[:, :, 0:1], 0.0))]

            def shifted(first):
                def consume(bv, f, n, tok):
                    s = ztr.next()
                    t = AC(s.ap[:, :, 1:257], bv, ACT.Copy, tok, s.free)
                    TT(zd, s.ap[:, :, 0:256], s.ap[:, :, 1:257], ALU.subtract, t)
                    for g in range(2):
                        z = first + f + g
                        t2 = STT(Z[:, z, :], zd[:, g, :], vc("mu", z), s.ap[:, g, 1:257], ALU.mult, ALU.add)
                    s.free = [t2]
                    return t
                return consume

            proj("in_wag", xs, shifted(0), t_xn)
            proj("in_rkv", xs, shifted(2))
            t_z = ve.last()
            zr, zk, zv = Z[:, 2:6, :], Z[:, 6:10, :], Z[:, 10:14, :]
            Vt = A.take(1024).rearrange("p (t f) -> p t f", t=2)
            qk = A.tiles(8)

            def ev_tok(dst):
                return lambda bv, tt, f, n, tok: ACi(dst[:, tt, f:f + n], bv, ACT.Copy, tok)

            def ev_cp(dst):
                return lambda bv, f, n, tok: ACi(dst[:, f:f + n, :], bv, ACT.Copy, tok)

            def ev_g(bv, f, n, tok):
                return AC(Gt[:, f:f + 2, :], bv, ACT.Sigmoid, tok)

            proj_tok("in_v", xs, ev_tok(Vt))
            proj("in_qk", xs, ev_cp(qk))
            dump("z", Z)

            ada2 = ada_steps(4, 12, ((ve, 0, 128), (po, 128, 512)), 1)
            next(ada2)
            t = AC(Z[0:64, 0, :], Z[0:64, 0, :], ACT.Tanh, t_z)
            t_w = t
            t_g = AC(Z[:, 1, :], Z[:, 1, :], ACT.Sigmoid)
            Gg = A.tiles(4)
            pe.wait(LD)
            for dst, lo, hi, z, off, bias in ((LDc, 0, 64, 0, 0, "w0"), (Aa, 64, 128, 0, 0, "a0"), (Gg, 0, 128, 1, 512, None)):
                for f in range(0, 4, 2):
                    b = bank()
                    for g in range(2):
                        tok = mm(b.ap[:, g * T:(g + 1) * T],
                                 [(lw[lo:hi, off + (f + g) * P:off + (f + g + 1) * P], Z[lo:hi, z, :])], t_w, t_g)
                    for g in range(2):
                        if bias:
                            b.free = [AC(dst[:, f + g, :], b.ap[:, g * T:(g + 1) * T], ACT.Sigmoid, tok,
                                         bias=vc(bias, f + g))]
                        else:
                            b.free = [AC(dst[:, f + g, :], b.ap[:, g * T:(g + 1) * T], ACT.Copy, tok)]
            t_lora = ac.last()
            Lc, EL = A.tiles(4), A.tiles(4)
            eml_at = A.at
            EmL, EP = A.tiles(4), A.tiles(4)
            TS(LDc, LDc, -float(np.exp(-0.5)), None, ALU.mult, None, t_lora)
            for k in range(4):
                ve.add(lambda e, k=k: e.tensor_tensor_scan(Lc[:, k, :], cst("reset"), LDc[:, k, :], 0.0,
                                                           ALU.mult, ALU.add))
            t = TT(EP, Lc, LDc, ALU.subtract)
            AC(EL, Lc, ACT.Exp, t)
            AC(EmL, Lc, ACT.Exp, scale=-1.0)
            t_e = AC(EP, EP, ACT.Exp)
            KK, Kt = A.tiles(4), A.tiles(4)
            bt_at = A.at
            Bt, tmp = A.tiles(4), Lc
            for k in range(4):
                TS(KK[:, k, :], zk[:, k, :], vc("k_k", k), None, ALU.mult, None)
            t = AC(tmp, KK, ACT.Square, ve.last())

            def blksum(src, o, scale, t):
                s2 = src.rearrange("p k t -> p (k t)")
                o2 = o.rearrange("p k t -> p (k t)")
                for f in range(2):
                    if f == 0:
                        next(ada2, None)
                    b = bank()
                    tk = mm(b.ap, [(blk, s2[:, f * 512:(f + 1) * 512])], t)
                    b.free = [TS(o2[:, f * 512:(f + 1) * 512], b.ap, scale, None, ALU.mult, None, tk)]
                return ve.last()

            RS4 = LDc
            blksum(tmp, RS4, 1.0, t)
            t = TS(RS4, RS4, 1e-24, None, ALU.max, None)
            t = AC(RS4, RS4, ACT.Sqrt, t)
            REC(RS4, RS4, t)
            TT(KK, KK, RS4, ALU.mult)
            TS(small[:, 16:20], vc("k_a", 0, 4), -1.0, 1.0, ALU.mult, ALU.add)
            for k in range(4):
                TS(tmp[:, k, :], Aa[:, k, :], vc("k_a", k), small[:, 16 + k:17 + k], ALU.mult, ALU.add)
            TT(Kt, zk, tmp, ALU.mult)
            TT(Bt, KK, Aa, ALU.mult)
            for k in range(4):
                t = STT(tmp[:, k, :], zr[:, k, :], vc("r_k", k), Kt[:, k, :], ALU.mult, ALU.mult)
            BON = Aa
            t = blksum(tmp, BON, 1.0, t)
            TT(BON, BON, zv, ALU.mult)
            al, be, kd, rd = EP, EmL, Kt, zr
            STT(al, KK, -1.0, EP, ALU.mult, ALU.mult, t_e)
            TT(kd, Kt, EmL, ALU.mult)
            TT(be, Bt, EmL, ALU.mult)
            t_rw = TT(rd, zr, EL, ALU.mult)
            dump("al", al)

            SQ8 = tmp
            SMALL_EL = small[:, 56:88].rearrange("p (k c) -> p k c", k=4)
            t_rw = CP(SMALL_EL, EL.rearrange("p k (c s) -> p k c s", s=32)[:, :, :, 31])
            qkf = A.tiles(8)
            for i, g in ((0, "qg"), (1, "kg")):
                v4 = qk[:, 4 * i:4 * i + 4, :]
                o4 = qkf[:, 4 * i:4 * i + 4, :]
                t = AC(SQ8, v4, ACT.Square, ve.last(), pe.last())
                blksum(SQ8, RS4, 1.0 / 64, t)
                TS(RS4, RS4, 1e-6, None, ALU.add, None)
                t = REC(RS4, RS4)
                t = AC(RS4, RS4, ACT.Sqrt, t)
                t = STT(v4, v4, vc(g), RS4, ALU.mult, ALU.mult, t)
                TT(o4, v4, bc(cA, 4), ALU.mult, t_rope)
                for f in range(0, 4, 2):
                    b = bank()
                    tk = mm(b.ap, [(cst("rotA"), qk[:, 4 * i + f:4 * i + f + 2, :])], t)
                    t2 = TT(SQ8[:, f:f + 2, :], b.ap.rearrange("p (n t) -> p n t", n=2), bc(sA, 2), ALU.mult, tk)
                    b.free = [t2]
                t_qk = TT(o4, o4, SQ8, ALU.add)
            Om = qk[:, 0:4, :]
            dump("qkf", qkf)

            def attention(mem, heads, dv, scale, parts, vof, base, evac, *w, step=None):
                sc = Buf([mem.take(384) for _ in range(3)])
                pt = Buf([mem.take(384) for _ in range(2)])
                st = {}

                def scores(h):
                    b = bank()
                    pe.wait(*w)
                    pr = parts(h)
                    mm(b.ap[:, 0:128], [(q[:, 0:128], k[:, 0:128]) for q, k in pr], signal=False)
                    tok = mm(b.ap[:, 128:384], [(q[:, 128:256], k[:, 0:256]) for q, k in pr])
                    s = sc.next()
                    STT(s.ap, b.ap[:, 0:384], scale, cst("mask3"), ALU.mult, ALU.add, tok, s.free)
                    b.free = [ve.last()]
                    n = small[:, 20 + 4 * (h % 4):24 + 4 * (h % 4)]
                    with ve.apart(ve.last()):
                        ve.add(lambda e: e.reduce_max(n[:, 0:1], s.ap[:, 0:128], AX.X, negate=True))
                        t = ve.add(lambda e: e.reduce_max(n[:, 1:2], s.ap[:, 128:384], AX.X, negate=True))
                    AC(s.ap[:, 0:128], s.ap[:, 0:128], ACT.Exp, t, bias=n[:, 0:1], accum_out=n[:, 2:3])
                    t = AC(s.ap[:, 128:384], s.ap[:, 128:384], ACT.Exp, bias=n[:, 1:2], accum_out=n[:, 3:4])
                    st[h] = (s, n, t)

                def weights(h):
                    s, n, t = st[h]
                    t = REC(n[:, 2:4], n[:, 2:4], t)
                    with ve.apart(t):
                        TS(s.ap[:, 0:128], s.ap[:, 0:128], n[:, 2:3], None, ALU.mult, None)
                        t = TS(s.ap[:, 128:384], s.ap[:, 128:384], n[:, 3:4], None, ALU.mult, None)
                    st[h] = (s, t)

                def turned(h):
                    s, t = st[h]
                    b = bank()
                    pe.wait(t)
                    for i in range(3):
                        tok = tr(b.ap[:, i * P:(i + 1) * P], s.ap[:, i * P:(i + 1) * P], signal=i == 2)
                    s.free = [tok]
                    p = pt.next()
                    t = AC(p.ap, b.ap[:, 0:384], ACT.Copy, tok, p.free)
                    b.free = [t]
                    st[h] = (p, t)

                def values(h):
                    p, t = st[h]
                    b = bank()
                    o = base(h)
                    mm(b.ap[o:o + dv, 0:256], [(vof(h, 0), p.ap[:, 0:256])], t, stop=False, signal=False)
                    tok = mm(b.ap[o:o + dv, 128:256], [(vof(h, 1), p.ap[:, 256:384])], start=False)
                    p.free = [tok]
                    b.free = [evac(h, b.ap[o:o + dv, 0:256], tok)]

                for i in range(heads + 3):
                    if 2 <= i < heads + 2:
                        weights(i - 2)
                    if i < heads:
                        scores(i)
                    if 2 <= i < heads + 2:
                        turned(i - 2)
                    if i >= 3:
                        values(i - 3)
                    if step:
                        step(i)

            def head(a, h):
                return a[64 * (h % 2):64 * (h % 2) + 64, h // 2, :]

            attention(att, 8, 64, 0.125, lambda h: [(head(qkf[:, 0:4, :], h), head(qkf[:, 4:8, :], h))],
                      lambda h, kt: Vt[:, kt, 64 * h:64 * h + 64], lambda h: 64 * (h % 2),
                      lambda h, b, tok: AC(head(Om, h), b, ACT.Copy, tok, t_qk), t_qk,
                      step=lambda i: next(ada2, None) if i % 2 else None)
            t_om = ac.last()
            for _ in ada2:
                pass
            dump("om", Om)

            barrier()
            free = [x.rearrange("p k t -> p (k t)") for x in (qkf, KK, Bt, Lc, LDc, zk, EL, qk[:, 4:8, :])]
            free += [Vt.rearrange("p t f -> p (t f)"), ar[:, A.at:ARENA], ar[:, 2 * SLOT:2 * SLOT + 1280],
                     ar[:, z_at - 768:z_at + 512], ar[:, z_at + 4096:att.hi]]
            free += [s.ap for s in asum.slots]
            used = [0] * len(free)

            def grab(n):
                for i, f in enumerate(free):
                    if f.shape[1] - used[i] >= n:
                        o = used[i]
                        used[i] += n
                        return f[:, o:o + n]
                raise ValueError(n)

            def grab4():
                return grab(512).rearrange("p (q t) -> p q t", q=4)

            ST = grab(2048).rearrange("p (c k i) -> p c k i", c=8, k=4)
            free.append(ar[:, SLOT:2 * SLOT])
            used.append(0)
            AR_ = [grab4() for _ in range(4)]
            Yy = grab(1024).rearrange("p (k t) -> p k t", k=4)
            toks4 = {}
            for nm, src in (("al", al), ("be", be), ("kd", kd), ("v", zv)):
                d = (zv.rearrange("p k t -> p (k t)") if nm == "v" else grab(1024)).rearrange("p (h f) -> p h f", h=2)
                bb = []
                for h in range(2):
                    b = bank()
                    pe.wait(t_rw)
                    for k in range(4):
                        tok = tr(b.ap[:, k * P:(k + 1) * P], src[:, k, h * P:(h + 1) * P], signal=k == 3)
                    bb.append(b)
                for h in range(2):
                    bb[h].free = [AC(d[:, h, :], bb[h].ap, ACT.Copy, tok)]
                toks4[nm] = d
            t_tok = ac.last()
            alT, beT, kdT, vT = (toks4[n] for n in ("al", "be", "kd", "v"))
            U0 = grab(1024).rearrange("p (h a k i) -> p h a k i", h=2, a=2, k=4)
            U = U0
            WT = grab(1024).rearrange("p (k t) -> p k t", k=4)
            places = [([grab4() for _ in range(8)], grab(256).rearrange("p (q i) -> p q i", q=4)) for _ in range(2)]

            def b4(b):
                return b.ap.rearrange("p (q t) -> p q t", q=4)

            def m4(name):
                return cst(name).unsqueeze(1).broadcast_to([P, 4, P])

            def quad(ls, rs, *w):
                b = bank()
                pe.wait(*w)
                for k in range(4):
                    tok = mm(b4(b)[:, k, :], [(ls(k), rs(k))], signal=k == 3)
                return b, tok

            def group(g):
                hf, par = g // 2, g % 2
                lo, ts = 64 * par, slice(hf * P, hf * P + P)
                (Xd, Xo, Yd, X2, Y2, R, Rn, Yk), XV = places[par]
                X4, Y4, AK = Xd, Yd, X2

                def sl(a):
                    return lambda k: a[lo:lo + 64, k, ts]

                def al4(a):
                    return lambda k: a[:, k, :]

                b, tk = quad(sl(al), sl(be), t_rw)
                TT(Xd, b4(b), m4("mXd"), ALU.mult, tk, pe.last())
                b.free = [TT(Xo, b4(b), m4("mXo"), ALU.mult)]
                yield
                b, tk = quad(sl(be), sl(al))
                t_yd = TT(Yd, b4(b), m4("mYd"), ALU.mult, tk)
                b.free = [t_yd]
                t_r1 = TT(R, Yd, m4("ident"), ALU.add)
                yield
                b, tk = quad(al4(Yd), al4(Xd), t_yd)
                bx = b, tk
                b2, tk2 = quad(al4(Xd), al4(Yd))
                yield
                b, tk = quad(sl(kd), sl(rd))
                t_ak = TT(AK, b4(b), m4("m32i"), ALU.mult, tk)
                b.free = [t_ak]
                b = bank()
                pe.wait(t_ak, t_tok)
                for k in range(4):
                    tk = mm(b4(b)[lo:lo + 64, k, :], [(vT[:, hf, k * P + lo:k * P + lo + 64], AK[:, k, :])],
                            signal=k == 3)
                b.free = [AC(Yy[lo:lo + 64, :, ts], b4(b)[lo:lo + 64, :, :], ACT.Copy, tk)]
                b, tk = bx
                b.free = [AC(X2, b4(b), ACT.Copy, tk, pe.last())]
                b2.free = [AC(Y2, b4(b2), ACT.Copy, tk2)]
                t_2 = ac.last()
                yield
                b, tk = quad(sl(kd), sl(al))
                b.free = [TT(Yk, b4(b), m4("m32s"), ALU.mult, tk)]
                t_yk = ve.last()
                yield
                b, tk = quad(al4(Y2), al4(X2), t_2)
                b.free = [AC(X4, b4(b), ACT.Copy, tk)]
                b, tk = quad(al4(X2), al4(Y2))
                b.free = [AC(Y4, b4(b), ACT.Copy, tk)]
                t_4 = ac.last()
                b, tk = quad(al4(X2), al4(R), t_r1)
                b.free = [TT(Rn, b4(b), R, ALU.add, tk)]
                t_r2 = ve.last()
                yield
                b, tk = quad(sl(be), sl(rd))
                b.free = [TT(AR_[g], b4(b), m4("m32i"), ALU.mult, tk)]
                yield
                b, tk = quad(al4(Y4), al4(X4), t_4)
                b.free = [AC(X2, b4(b), ACT.Copy, tk)]
                t_8 = ac.last()
                b, tk = quad(al4(X4), al4(Rn), t_r2)
                b.free = [TT(R, b4(b), Rn, ALU.add, tk)]
                t_r3 = ve.last()
                yield
                b = bank()
                pe.wait(t_tok, t_yk)
                for k in range(4):
                    tk = mm(b.ap[:, k * 64:k * 64 + 64],
                            [(Yk[:, k, :], vT[:, hf, k * P + lo:k * P + lo + 64])], signal=k == 3)
                b.free = [AC(XV, b.ap[:, 0:256].rearrange("p (q i) -> p q i", q=4), ACT.Copy, tk)]
                t_xv = ac.last()
                yield
                b, tk = quad(al4(X2), al4(R), t_8, t_r3)
                b.free = [TT(Rn, b4(b), R, ALU.add, tk)]
                t_r4 = ve.last()
                yield
                b = bank()
                pe.wait(t_r4)
                for k in range(4):
                    tk = tr(b4(b)[:, k, :], Rn[:, k, :], signal=k == 3)
                b.free = [AC(X4, b4(b), ACT.Copy, tk)]
                b, tk = quad(al4(Xo), al4(Rn))
                b.free = [AC(Y4, b4(b), ACT.Copy, tk)]
                t_m = ac.last()
                yield
                b, tk = quad(al4(X4), al4(Y4), t_m)
                b.free = [TT(R, b4(b), Rn, ALU.add, tk)]
                t_r5 = ve.last()
                yield
                b = bank()
                pe.wait(t_xv, t_r5)
                for k in range(4):
                    tk = mm(b.ap[:, k * 64:k * 64 + 64], [(R[:, k, :], XV[:, k, :])], signal=k == 3)
                b.free = [CP(U0[:, hf, par, :, :], b.ap[:, 0:256].rearrange("p (q i) -> p q i", q=4), tk)]
                b = bank()
                for k in range(4):
                    tk = mm(b4(b)[lo:lo + 64, k, :], [(alT[:, hf, k * P + lo:k * P + lo + 64], R[:, k, :])],
                            signal=k == 3)
                b.free = [AC(WT[lo:lo + 64, :, ts], b4(b)[lo:lo + 64, :, :], ACT.Copy, tk)]
                yield

            for hf in range(2):
                for _ in zip(group(2 * hf), group(2 * hf + 1)):
                    pass
            dump("ar", AR_[0])
            t_yv = ac.last()
            t_u0 = [ve.add(lambda e: e.memset(ST[:, 0, :, :], 0.0)), ac.last()]
            t_s = t_u0
            tS = places[0][1]
            for c in range(8):
                hf, rb = c // 4, 32 * (c % 4)
                cs = slice(c * 32, c * 32 + 32)

                def outer(bs, lhs, rhs, start):
                    for k in range(4):
                        for par in range(2):
                            f = slice(k * P + 64 * par, k * P + 64 * par + 64)
                            r = rhs(par, k, f)
                            tk = mm(bs.ap[64 * par:64 * par + 64, k * 64:k * 64 + 64], [(lhs[rb:rb + 32, hf, f], r)],
                                    start=start and k == 0, stop=not start, signal=k == 3 and par == 1, skip=True)
                    return tk

                if c < 7:
                    bs = bank()
                    outer(bs, kdT, lambda par, k, f: vT[rb:rb + 32, hf, f], True)
                for par in range(2):
                    lo = 64 * par
                    b = bank()
                    pe.wait(t_s)
                    for k in range(4):
                        tk = mm(b.ap[rb:rb + 32, k * 64:k * 64 + 64], [(WT[lo:lo + 64, k, cs], ST[lo:lo + 64, c, k, :])],
                                signal=k == 3)
                    with ve.apart():
                        t_ = TT(U[rb:rb + 32, hf, par, :, :], b.ap[rb:rb + 32, 0:256].rearrange("p (q i) -> p q i", q=4),
                                U0[rb:rb + 32, hf, par, :, :], ALU.add, tk, t_u0)
                    b.free = [t_]
                if c == 7:
                    break
                pe.wait(ve.last())
                b = bs
                tk = outer(bs, beT, lambda par, k, f: U[rb:rb + 32, hf, par, k, :], False)
                b.free = [TT(tS, b.ap[:, 0:256].rearrange("p (q i) -> p q i", q=4), ST[:, c, :, :], ALU.add, tk)]
                t_s = TT(ST[:, c + 1, :, :], tS, SMALL_EL[:, :, c:c + 1].broadcast_to([P, 4, 64]), ALU.mult)
            t_u = ve.last()
            for g in range(4):
                hf, par = g // 2, g % 2
                lo, ts = 64 * par, slice(hf * P, hf * P + P)
                b = bank()
                pe.wait(t_u)
                for k in range(4):
                    o = b.ap[lo:lo + 64, k * P:(k + 1) * P]
                    f = slice(k * P + lo, k * P + lo + 64)
                    mm(o, [(U[:, hf, par, k, :], AR_[g][:, k, :])], stop=False, signal=False)
                    for c in range(4):
                        tk = mm(o[:, c * 32:c * 32 + 32],
                                [(ST[lo:lo + 64, 4 * hf + c, k, :], rd[lo:lo + 64, k, hf * P + c * 32:hf * P + c * 32 + 32])],
                                start=False, stop=c == 3, signal=k == 3 and c == 3)
                b.free = [TT(Yy[lo:lo + 64, :, ts], b4(b)[lo:lo + 64, :, :], Yy[lo:lo + 64, :, ts], ALU.add, tk, t_yv)]
            dump("y", Yy)
            M4, S4 = al, be
            slots["extra"][1] = [pe.last(), ve.last(), ac.last()]
            proj("in_g", xs, ev_g)
            blksum(Yy, M4, 1.0 / 64, ve.last())
            t = TT(Yy, Yy, M4, ALU.subtract)
            t = AC(S4, Yy, ACT.Square, t)
            blksum(S4, M4, 1.0 / 64, t)
            TS(M4, M4, 64e-5, None, ALU.add, None)
            t = REC(M4, M4)
            t = AC(M4, M4, ACT.Sqrt, t)
            TT(Yy, Yy, M4, ALU.mult, t)
            for k in range(4):
                TS(Yy[:, k, :], Yy[:, k, :], vc("ln_g", k), vc("ln_b", k), ALU.mult, ALU.add)
            TT(Yy, Yy, BON, ALU.add)
            t_or = TT(Yy, Yy, Gg, ALU.mult)
            dump("orw", Yy)

            oms, t_om = split_act(Om, 8, t_om)
            ors, t_or = split_act(Yy, 12, t_or)
            MIX = ar[:, eml_at:eml_at + 2048].rearrange("p (k t) -> p k t", k=8)
            mA = Buf([kd[:, 2 * i:2 * i + 2, :] for i in range(2)])
            t_g = ac.last()
            mps = []
            for name, src in (("pm", oms), ("pr", ors)):
                def ev_mix(bv, f, n, tok, name=name):
                    g = Gt[:, f:f + n, :] if name == "pm" else Gt[:, 8 + f:8 + f + n, :]
                    if name == "pm":
                        return TT(MIX[:, f:f + n, :], bv, g, ALU.mult, tok, t_g)
                    m = mA.next()
                    t = TT(m.ap, bv, g, ALU.mult, tok, t_g)
                    TT(MIX[:, f:f + n, :], MIX[:, f:f + n, :], m.ap, ALU.add)
                    return t
                proj(name, src, ev_mix, t_om, t_or)
            xs, t = split_act(MIX, 0, ve.last())

            def ev_h(bv, f, n, tok):
                for g in range(n):
                    t = STT(X[:, f + g, :], bv[:, g, :], mod[:, 16 + f + g:17 + f + g], X[:, f + g, :],
                            ALU.mult, ALU.add, tok)
                return t

            proj("wo", xs, ev_h, t)
            dump("h", X)
            barrier()
            slots["use"] = [0, 1, 2]
            slots["extra"][2] = [q.last() for q in (pe, ve, ac)]

            H2 = ar[:, BASE:BASE + 64 * T].rearrange("p (b i t) -> p b i t", b=2, i=32)
            B = Arena(ar, BASE + 64 * T, ARENA)
            idT = B.take(3 * T).rearrange("p (a t) -> p a t", a=3)
            Bq = Arena(ar, BASE + 32 * T, ARENA)
            Qp = Bq.tiles(16)
            sq = Qp[:, 0:8, :]
            rs = Qp[:, 8, :]
            t = AC(sq, X, ACT.Square)
            b, t = colsum(sq, 8, t)
            t_r = rstd_of(rs, b.ap[:, 0:T], 1.0 / 1024, 1e-6, t)
            b.free = [ve.last()]
            TT(sq, X, bc(rs, 8), ALU.mult, t_r)
            STT(mod[:, 48:56], mod[:, 32:40], 1.0, vc("n2", 0, 8), ALU.add, ALU.mult)
            for k in range(8):
                t = TS(sq[:, k, :], sq[:, k, :], mod[:, 48 + k:49 + k], mod[:, 24 + k:25 + k], ALU.mult, ALU.add)
            dump("xn2", sq)
            xs, t_xn = split_act(sq, 0, t)
            proj("wq", xs, ev_cp(Qp), t_xn)
            t_q = ac.last()
            sub = take("sub", 0)
            pe.wait(sub.tok, t_q)
            M = Arena(ar, BASE + 32 * T + 4096, BASE + 64 * T)
            S = M.take(4096).rearrange("p (a g n) -> p a g n", a=2, g=16)
            M = Arena(ar, BASE + 32 * T, BASE + 32 * T + 4096)
            for tt in range(2):
                for g in range(0, 16, 4):
                    b = bank()
                    for k in range(4):
                        tk = mm(b.ap[:, k * P:(k + 1) * P], [(Qp[:, g + k, tt * P:(tt + 1) * P],
                                                              sub.flat[:, (g + k) * P:(g + k + 1) * P])], signal=k == 3)
                    sub.chunk.free = [tk]
                    b.free = [AC(S[:, tt, g:g + 4, :], b.ap.rearrange("p (q n) -> p q n", q=4), ACT.Copy, tk)]
            t_S = ac.last()
            cand = M.take(2048).rearrange("p (h x) -> p h x", h=8)
            top = M.take(256).rearrange("p (g k) -> p g k", g=16)
            ti = M.take(256).bitcast(U32).rearrange("p (g k) -> p g k", g=16)
            tif = M.take(256).rearrange("p (h a k) -> p h a k", h=8, a=2)
            bs_ = M.take(128).rearrange("p (h k) -> p h k", h=8)
            bj = M.take(128).bitcast(U32).rearrange("p (h k) -> p h k", h=8)
            raw = M.take(128).bitcast(U32)
            fi = M.take(128)
            M = Arena(ar, B.at, ARENA)
            res = [[M.take(128) for _ in range(3)] for _ in range(2)]
            ve.wait(t_S, pe.last())

            def top16(rows, *w):
                toks = [list(w)] * len(rows)
                for r in range(2):
                    s8 = slice(8 * r, 8 * r + 8)
                    for i, (src, vals, idx) in enumerate(rows):
                        toks[i] = ve.add(lambda e, src=src, v=vals[:, s8]: e.max(v, src), toks[i])
                    for i, (src, vals, idx) in enumerate(rows):
                        toks[i] = ve.add(lambda e, src=src, v=vals[:, s8], x=idx[:, s8]: e.max_index(x, v, src), toks[i])
                    if r == 0:
                        for i, (src, vals, idx) in enumerate(rows):
                            toks[i] = ve.add(lambda e, src=src, v=vals[:, s8]: e.match_replace(src, v, src, -3.0e38),
                                             toks[i])

            def routing():
                for tt in range(2):
                    for g in range(0, 16, 4):
                        with ve.apart(ve.last()):
                            top16([(S[:, tt, x, :], top[:, x, :], ti[:, x, :]) for x in range(g, g + 4)])
                        yield
                    CP(tif.rearrange("p h a k -> p (h a k)"), ti.rearrange("p g k -> p (g k)"))
                    tv = top.rearrange("p (h a) k -> p h a k", a=2)
                    for h in range(0, 8, 4):
                        with ve.apart(ve.last()):
                            for x in range(h, h + 4):
                                t = TT(cand[:, x, :].rearrange("p (a b) -> p a b", a=16),
                                       tv[:, x, 0, :].unsqueeze(2).broadcast_to([P, 16, 16]),
                                       tv[:, x, 1, :].unsqueeze(1).broadcast_to([P, 16, 16]), ALU.add)
                            top16([(cand[:, x, :], bs_[:, x, :], bj[:, x, :]) for x in range(h, h + 4)], t)
                        yield
                    gf = res[tt][2]
                    g_ = gf.rearrange("p (h k) -> p h k", h=8)
                    t = TT(g_, bs_, bs_[:, :, 0:1].broadcast_to([P, 8, 16]), ALU.subtract)
                    t = AC(g_, g_, ACT.Exp, t)
                    ve.add(lambda e, g_=g_: e.reduce_sum(small[:, 40:48], g_, AX.X), t)
                    REC(small[:, 40:48], small[:, 40:48])
                    TT(g_, g_, small[:, 40:48].unsqueeze(2).broadcast_to([P, 8, 16]), ALU.mult)
                    yield
                    bju = bj.rearrange("p h k -> p (h k)")
                    oh = cand.rearrange("p h x -> p (h x)")
                    o3 = oh.rearrange("p (x k) -> p x k", k=16)
                    for a in range(2):
                        if a == 0:
                            ve.add(lambda e: e.tensor_single_scalar(raw, bju, 4, ALU.logical_shift_right))
                        else:
                            ve.add(lambda e: e.tensor_single_scalar(raw, bju, 15, ALU.bitwise_and))
                        CP(fi, raw)
                        TT(o3, fi.unsqueeze(2).broadcast_to([P, 128, 16]),
                           cst("iota", 0, 16).unsqueeze(1).broadcast_to([P, 128, 16]), ALU.is_equal)
                        yield
                        with ve.apart(ve.last()):
                            for h in range(8):
                                o2 = oh[:, h * 256:(h + 1) * 256].rearrange("p (x k) -> p x k", k=16)
                                TT(o2, o2, tif[:, h, a, :].unsqueeze(1).broadcast_to([P, 16, 16]), ALU.mult)
                        yield
                        ve.add(lambda e, a=a, tt=tt: e.reduce_sum(res[tt][a], o3, AX.X))
                        yield

            ohj = Buf([RH[:, 12 + 2 * i:14 + 2 * i, :].rearrange("p k (a j) -> p (k a) j", a=2) for i in range(2)])
            ohi = Buf([RL[:, 12 + 2 * i:14 + 2 * i, :].rearrange("p k (x a i) -> p (k x) a i", x=4, a=2) for i in range(2)])
            eqb = Buf([B.take(256).rearrange("p (x i) -> p x i", x=8) for _ in range(2)])
            HG = Buf([(RH[:, 8 + 2 * i:10 + 2 * i, :], RL[:, 8 + 2 * i:10 + 2 * i, :]) for i in range(2)])
            gg = B.take(2 * T).rearrange("p (t a) -> p t a", a=2)
            gsum = Buf([B.take(256).rearrange("p (t i) -> p t i", t=8) for _ in range(2)])
            acc = banks[4:8]
            pool_banks[0], pool_banks[1] = [0, 1, 2, 3], 0
            t_H = [[], []]

            def up(b_):
                for g in range(8):
                    for pi in range(2):
                        it = take("u", b_ * 8 + g, pi)
                        b = bank()
                        bv = b.ap.rearrange("p (n t) -> p n t", n=2)
                        pe.wait(it.tok)
                        for n in range(2):
                            fs = slice(n * P, (n + 1) * P)
                            for a in (0, 4):
                                tk = mm3(bv[:, n, :], [(it.h[:, k, fs], it.l[:, k, fs], xs[0][:, k, :], xs[1][:, k, :])
                                                       for k in range(a, a + 4)],
                                         start=a == 0, stop=a == 4, signal=n == 1 and a == 4)
                                if not (n == 1 and a == 4):
                                    yield
                        it.done = tk
                        i0 = g * 4 + pi * 2
                        t = ACi(H2[:, b_ % 2, i0:i0 + 2, :], bv, ACT.Gelu, tk, t_H[b_ % 2])
                        b.free = [t]
                        yield
                t_H[b_ % 2] = [t]

            def gate(b_, alone=True):
                Hb = H2[:, b_ % 2, :, :]
                rows = {}

                def build(t):
                    if t % 8 == 0:
                        oi, eq = ohi.next(), eqb.next()
                        with ve.apart(t_id):
                            x = TT(eq.ap, cst("iota", 32 * b_, 32 * b_ + 32).unsqueeze(1).broadcast_to([P, 8, 32]),
                                   idT[:, 0, t:t + 8].unsqueeze(2).broadcast_to([P, 8, 32]), ALU.is_equal, eq.free)
                            y = TT(oi.ap, eq.ap.unsqueeze(2).broadcast_to([P, 8, 2, 32]),
                                   gg[:, t:t + 8, :].unsqueeze(3).broadcast_to([P, 8, 2, 32]), ALU.mult, x, oi.free)
                            eq.free = [y]
                        rows["i"] = (oi, y)
                    oj = ohj.next()
                    if alone:
                        with po.apart(t_id):
                            for j in range(4):
                                z = TS(oj.ap[:, j, :], cst("iota"), idT[:, 1, t + j:t + j + 1], None,
                                       ALU.is_equal, None, oj.free, q=po)
                    else:
                        with ve.apart(t_id):
                            z = TT(oj.ap, cst("iota").unsqueeze(1).broadcast_to([P, 4, P]),
                                   idT[:, 1, t:t + 4].unsqueeze(2).broadcast_to([P, 4, P]), ALU.is_equal, oj.free)
                    rows[t] = rows["i"] + (oj, z)

                build(0)
                for t in range(0, T, 4):
                    if t + 4 < T:
                        build(t + 4)
                    if t % 8 == 0:
                        b = bank()
                    oi, y, oj, z = rows.pop(t)
                    for j in range(4):
                        c = (t % 8 + j) * 64
                        tk = mm(b.ap[:, c:c + 64], [(oj.ap[:, j, :], oi.ap[:, t % 8 + j, :, :])], y, z, signal=j == 3)
                    oi.free = oj.free = [tk]
                    if t % 8 == 4:
                        hv = Hb[:, :, t - 4:t + 4].rearrange("p i t -> p t i")
                        g2 = b.ap.rearrange("p (t a i) -> p t a i", t=8, a=2)
                        s = gsum.next()
                        with ve.apart():
                            x = ACi(s.ap, g2[:, :, 0, :], ACT.Copy, tk, s.free)
                            x = TT(s.ap, s.ap, g2[:, :, 1, :], ALU.add, x)
                            b.free = [x]
                            x = TT(hv, hv, s.ap, ALU.mult, x, t_H[b_ % 2])
                        s.free = [x]
                    yield
                t_H[b_ % 2] = [x]

            def down(b_):
                def pair(q):
                    hg = HG.next()
                    src = H2[:, b_ % 2, 2 * q:2 * q + 2, :]
                    t = ACi(hg.ap[0], src, ACT.Copy, t_H[b_ % 2], hg.free)
                    with lo_on[0].apart():
                        t = TT(hg.ap[1], src, hg.ap[0].bitcast(F32), ALU.subtract, t, t_H[b_ % 2], hg.free, q=lo_on[0])
                    return hg, t

                nxt = pair(0)
                for q in range(16):
                    it = take("v", b_ * 8 + q // 2, q % 2)
                    hg, t = nxt
                    if q < 15:
                        nxt = pair(q + 1)
                    pe.wait(it.tok, t)
                    for n in range(2):
                        for tt in range(2):
                            ts = slice(tt * P, (tt + 1) * P)
                            for dh in range(2):
                                ds = slice(dh * 512, dh * 512 + 512)
                                tk = mm3(acc[tt * 2 + dh].ap,
                                         [(hg.ap[0][:, n, ts], hg.ap[1][:, n, ts], it.h[:, n, ds], it.l[:, n, ds])],
                                         start=b_ == 0 and q == 0 and n == 0, stop=b_ == 3 and q == 15 and n == 1,
                                         signal=n == 1 and tt == 1 and dh == 1)
                            if n == 0 or tt == 0:
                                yield
                    hg.free = [tk]
                    it.done = tk
                    yield
                t_H[b_ % 2] = [ve.last(), po.last()]

            def beside(main, side, ratio):
                due = 0.0
                for _ in main:
                    due += ratio
                    while due >= 1:
                        due -= 1
                        next(side, None)

            def finish(side):
                for _ in side:
                    pass

            lo_on[0] = po
            r = routing()
            beside(up(0), r, 0.36)
            finish(r)
            lo_on[0] = ve
            b = bank()
            b2 = bank()
            pe.wait(ve.last())
            for tt, bb in ((0, b), (1, b2)):
                for i in range(3):
                    tk = tr(bb.ap[:, i * P:(i + 1) * P], res[tt][i], signal=i == 2)
                bb.free = [CP(idT[:, :, tt * P:(tt + 1) * P], bb.ap[:, 0:384].rearrange("p (a t) -> p a t", a=3), tk)]
            ghr = RH[:, 12, :]
            CP(ghr, idT[:, 2, :])
            CP(gg[:, :, 0], ghr.bitcast(F32))
            t_id = TT(gg[:, :, 1], idT[:, 2, :], ghr.bitcast(F32), ALU.subtract)
            dump("idT", idT)
            pe.wait(*[b.free for b in acc])
            lo_on[0] = po
            g0 = gate(0, False)
            beside(up(1), g0, 1.0)
            finish(g0)
            lo_on[0] = ve
            g1 = gate(1)
            beside(down(0), g1, 0.5)
            beside(up(2), g1, 0.5)
            finish(g1)
            g2 = gate(2)
            beside(down(1), g2, 0.5)
            beside(up(3), g2, 0.5)
            finish(g2)
            lo_on[0] = po
            g3 = gate(3, False)
            beside(down(2), g3, 1.0)
            finish(g3)
            lo_on[0] = ve
            finish(down(3))
            t_acc = pe.last()
            prev_mul = ve.last()
            ot = ar[:, BASE:BASE + 2048].rearrange("p (t d) -> p t d", t=2)
            for tt in range(2):
                for dh in range(2):
                    q = AC if dh else None
                    o = ot[:, tt, dh * 512:dh * 512 + 512]
                    src = acc[tt * 2 + dh]
                    if dh:
                        src.free = [AC(o, src.ap, ACT.Copy, t_acc, prev_mul)]
                    else:
                        src.free = [CP(o, src.ap, t_acc)]
            tw = [ve.last(), ac.last()]
            for k in range(0, 8, 2):
                b = bank()
                pe.wait(tw)
                for g in range(2):
                    for tt in range(2):
                        tk = tr(b.ap[:, g * T + tt * P:g * T + (tt + 1) * P], ot[:, tt, (k + g) * P:(k + g + 1) * P],
                                signal=g == 1 and tt == 1)
                for g in range(2):
                    b.free = [STT(X[:, k + g, :], b.ap[:, g * T:(g + 1) * T], mod[:, 40 + k + g:41 + k + g],
                                  X[:, k + g, :], ALU.mult, ALU.add, tk)]
            pool_banks[0], pool_banks[1] = list(range(8)), 0
            dump("h1", X)
            barrier()

            B = Arena(ar, BASE, ARENA)
            K2B = B.take(512)
            keep = B.at
            K2 = B.take(2048)
            ac.add(lambda e: e.dma_start(K2[:, 0:512], D["con2"][:, 0:512]).then_inc(s_ld2, 16), signal=False)
            ac.add(lambda e: e.dma_start(K2B, D["con2"][:, 512:1024]).then_inc(s_ld2, 16), signal=False)
            ac.add(lambda e: e.dma_start(K2[:, 512:2048], D["con2"][:, 1024:2560]).then_inc(s_ld2, 16), signal=False)
            LD2 = (s_ld2, 48)
            cosA, sinA, dec = K2[:, 0:T], K2[:, T:2 * T], K2[:, 512:2048]
            cosB, sinB = K2B[:, 0:T], K2B[:, T:2 * T]
            xs, t_xs = split_act(X, 0)
            QK = B.tiles(16)
            V2 = B.take(4096).rearrange("p (t f) -> p t f", t=2)
            Gs = B.tiles(16)
            tb = Buf([B.tiles(4) for _ in range(2)])

            def ev_rope(bv, f, n, tok):
                h, i = (f // 2) % 4, f // 8
                o = QK[:, 4 * h + 2 * i:4 * h + 2 * i + 2, :]
                s = tb.next()
                TT(s.ap[:, 0:2, :], bv, bc(cosA, 2), ALU.mult, tok, LD2)
                t = TT(s.ap[:, 2:4, :], bv, bc(sinA, 2), ALU.mult)
                TT(o[:, 0, :], s.ap[:, 0, :], s.ap[:, 3, :], ALU.subtract)
                TT(o[:, 1, :], s.ap[:, 1, :], s.ap[:, 2, :], ALU.add)
                return t

            sgb = Buf([B.tiles(2) for _ in range(2)])

            def ev_silu(bv, f, n, tok):
                s = sgb.next()
                t = AC(s.ap, bv, ACT.Sigmoid, tok, s.free)
                t = TT(Gs[:, f:f + 2, :], bv, s.ap, ALU.mult, t)
                s.free = [t]
                return t

            proj("a_qk", xs, ev_rope, t_xs)
            t_qk = ve.last()
            proj_tok("a_v", xs, ev_tok(V2))
            t_v = ac.last()
            O2 = QK
            PTb = Buf([B.take(384) for _ in range(2)])
            gst = proj_steps("a_g", xs, ev_silu)
            t_oh = []
            for h in range(4):
                b = bank()
                pe.wait(t_qk, t_v)
                q, k = QK[:, 4 * h:4 * h + 2, :], QK[:, 4 * h + 2:4 * h + 4, :]
                mm(b.ap[:, 0:256], [(k[:, d, 0:128], q[:, d, :]) for d in range(2)], signal=False)
                tk = mm(b.ap[:, 256:384], [(k[:, d, 128:256], q[:, d, 128:256]) for d in range(2)])
                p = PTb.next()
                t = TT(p.ap, b.ap[:, 0:384], dec[:, h * 384:(h + 1) * 384], ALU.mult, tk, p.free)
                b.free = [t]
                for f in range(0, 4, 2):
                    b = bank()
                    pe.wait(t)
                    for g in range(2):
                        c = h * 512 + (f + g) * P
                        mm(b.ap[:, g * T:(g + 1) * T], [(V2[:, 0, c:c + P], p.ap[:, 0:256])], stop=False, signal=False)
                        tk = mm(b.ap[:, g * T + P:(g + 1) * T], [(V2[:, 1, c:c + P], p.ap[:, 256:384])], start=False,
                                signal=g == 1)
                    b.free = [AC(O2[:, 4 * h + f:4 * h + f + 2, :], b.ap.rearrange("p (n t) -> p n t", n=2),
                                 ACT.Copy, tk)]
                p.free = [tk]
                t_oh.append(ac.last())
            mean, rsd = B.take(T), B.take(T)

            def normalise(x, nk, eps, sqbuf, *w, steps=None):
                b, t = colsum(x, nk, *w)
                b.free = [TS(mean, b.ap[:, 0:T], 1.0 / (nk * P), None, ALU.mult, None, t)]
                if steps is not None:
                    next(steps, None)
                t = TT(x, x, bc(mean, nk), ALU.subtract)
                t = AC(sqbuf, x, ACT.Square, t)
                if steps is not None:
                    next(steps, None)
                b, t = colsum(sqbuf, nk, t)
                t = rstd_of(rsd, b.ap[:, 0:T], 1.0 / (nk * P), eps, t)
                b.free = [ve.last()]
                return TT(x, x, bc(rsd, nk), ALU.mult, t)

            for h in range(4):
                s_ = tb.next()
                normalise(O2[:, 4 * h:4 * h + 4, :], 4, 1e-5, s_.ap, t_oh[h], ve.last(), steps=gst)
            finish(gst)
            t = TT(O2, O2, Gs, ALU.mult, pe.last())
            os_, t = split_act(O2, 0, t)
            dump("o2", O2)
            alpha = float(4.0 ** 0.25)

            def ev_res(bv, f, n, tok):
                return STT(X[:, f:f + n, :], X[:, f:f + n, :], alpha, bv, ALU.mult, ALU.add, tok)

            def layer_norm(l, sqbuf):
                normalise(X, 8, 1e-5, sqbuf, ve.last())
                with ve.apart(ve.last()):
                    for k in range(8):
                        t = TS(X[:, k, :], X[:, k, :], vc("g2", 8 * l + k), vc("b2", 8 * l + k), ALU.mult, ALU.add)
                return t

            proj("a_o", os_, ev_res, t)
            t_x = layer_norm(0, QK[:, 0:8, :])
            xs, t_xs = split_act(X, 0, t_x)
            dump("x1", X)
            barrier()

            B = Arena(ar, keep, ARENA)
            kr = B.tiles(2)
            Kn = B.tiles(16)
            V3 = B.take(4096).rearrange("p (t f) -> p t f", t=2)
            Qr = B.tiles(8)
            qn_at = B.at
            Qn = B.tiles(16)
            Bn = Arena(ar, qn_at, B.at)
            lat, Ql, sq6 = Bn.tiles(4), Bn.tiles(6), Bn.tiles(6)
            rsd = B.take(T)
            mean = B.take(T)
            sr = B.tiles(2)
            sgb = Buf([B.tiles(2) for _ in range(2)])

            proj("kvd", xs, ev_cp(lat), t_xs)
            proj("kvr", xs, ev_cp(kr))
            t_kr = ac.last()
            proj("b_q4", xs, ev_cp(Ql))
            proj("b_q2", xs, ev_cp(Ql[:, 4:6, :]))

            def rms(x, nk, gname, *w):
                t = AC(sq6[:, 0:nk, :], x, ACT.Square, ve.last(), pe.last(), *w)
                b, t = colsum(sq6, nk, t)
                t = rstd_of(rsd, b.ap[:, 0:T], 1.0 / (nk * P), 1e-6, t)
                b.free = [ve.last()]
                with ve.apart(t, ve.last()):
                    for k in range(nk):
                        t = STT(x[:, k, :], x[:, k, :], vc(gname, k), rsd, ALU.mult, ALU.mult)
                return t

            t_lat = rms(lat, 4, "kvn")
            lats, t_lat = split_act(lat, 8, t_lat)

            def rotB(x, n, o, tok):
                b = bank()
                bv = b.ap[:, 0:n * T].rearrange("p (n t) -> p n t", n=n)
                tk = mm(bv, [(cst("rotB"), x)], tok)
                s = sr[:, 0:n, :]
                t = TT(s, bv, bc(sinB, n), ALU.mult, tk)
                b.free = [t]
                TT(o, x, bc(cosB, n), ALU.mult)
                return TT(o, o, s, ALU.add)

            rotB(kr[:, 0:1, :], 1, kr[:, 1:2, :], t_kr)
            proj("kvk", lats, ev_cp(Kn), t_lat)
            t_qn = rms(Ql, 6, "bq")
            proj_tok("kvv", lats, ev_tok(V3))
            qls, t_qn = split_act(Ql, 8, t_qn)
            proj("uqn", qls, ev_cp(Qn), t_qn)
            proj("uqr", qls, ev_cp(Qr))
            t = ac.last()
            for f in range(0, 8, 2):
                t_rq = rotB(Qr[:, f:f + 2, :], 2, Qr[:, f:f + 2, :], t)
            t_kn = t
            dump("qr", Qr)
            O3 = Qn
            t_ev = {}

            def evac3(h, b, tok):
                t_ev[h] = AC(O3[:, h, :], b, ACT.Copy, tok)
                return t_ev[h]

            def parts3(h):
                lo = 64 * (h % 2)
                return [(Qn[:, h, :], Kn[:, h, :]), (Qr[lo:lo + 64, h // 2, :], kr[lo:lo + 64, 1, :])]

            def ev_gate(bv, f, n, tok):
                s = sgb.next()
                t = AC(s.ap, bv, ACT.Sigmoid, tok, s.free)
                t = TT(s.ap, bv, s.ap, ALU.mult, t)
                s.free = [TT(O3[:, f:f + 2, :], O3[:, f:f + 2, :], s.ap, ALU.mult, t_ev[f + 1])]
                return t

            gst = proj_steps("b_g", xs, ev_gate)

            def between(i):
                if i >= 5 and i % 2 == 1:
                    next(gst, None)

            attention(B, 16, 128, float(192.0 ** -0.5), parts3, lambda h, kt: V3[:, kt, h * P:(h + 1) * P],
                      lambda h: 0, evac3, t_rq, t_kn, step=between)
            finish(gst)
            dump("o3", O3)
            os_, t = split_act(O3, 0, ve.last(), ac.last())
            proj("b_o", os_, ev_res, t)
            layer_norm(1, V3.rearrange("p t f -> p (t f)")[:, 0:2048].rearrange("p (k t) -> p k t", k=8))
            dump("xf", X)

        try:
            stages()
        except Stop:
            pass
        fin = [q.last() for q in (pe, ve, ac, po) if q.n]
        sp_out = fin

        if dry:
            return items_order
        for c in chunks:
            if c.before is not None:
                sp.wait(c.before.free)
            sp.wait(c.wait)
            sp.add(lambda e, c=c: e.dma_start(c.flat, D[c.name][c.j]).then_inc(slot_sem[c.slot], 16), signal=False)
        sp.wait(LDX, LD, *sp_out)
        sp.add(lambda e: e.dma_start(out, Xt[:, :]).then_inc(s_out, 16), signal=False)
        sp.wait((s_out, 16))

        block = ctx.enter_context(nc.Block())

        @block.sync
        def _(e):
            sp.run(e)

        @block.scalar
        def _(e):
            ac.run(e)

        @block.vector
        def _(e):
            ve.run(e)

        @block.gpsimd
        def _(e):
            po.run(e)

        @block.tensor
        def _(e):
            pe.run(e)


def constants():
    a = np.zeros((P, C1W), np.float32)

    def put(name, v):
        o, w = C1[name]
        a[:, o:o + w] = v

    r = np.arange(P)
    row, col = r[:, None], r[None, :]
    put("ident", np.eye(P))
    put("ones", 1.0)
    put("blk", row // 64 == col // 64)
    rot = np.zeros((P, P))
    for h in range(2):
        for d in range(8):
            rot[64 * h + d + 8, 64 * h + d] = -1
            rot[64 * h + d, 64 * h + d + 8] = 1
    put("rotA", rot)
    rot = np.zeros((P, P))
    for h in range(2):
        for d in range(32):
            rot[64 * h + d + 32, 64 * h + d] = -1
            rot[64 * h + d, 64 * h + d + 32] = 1
    put("rotB", rot)
    put("mXd", (row // 16 == col // 16) & (col < row))
    put("mXo", (row // 32 == col // 32) & (row // 16 != col // 16) & (col < row))
    put("mYd", (row // 16 == col // 16) & (row < col))
    put("m32s", (row // 32 == col // 32) & (row < col))
    put("m32i", (row // 32 == col // 32) & (row <= col))
    tri = np.where(col <= row, 0.0, NEG)
    put("mask3", np.concatenate([tri, np.zeros((P, P)), tri], 1))
    put("reset", (np.arange(256) % 32 != 0)[None, :] * np.ones((P, 1)))
    put("iota", col * np.ones((P, 1)))
    inv = np.zeros(P, np.float32)
    e = np.float32(500000.0) ** (-(np.arange(8, dtype=np.float32) * np.float32(2.0)) / np.float32(16))
    for h in range(2):
        for s in range(2):
            inv[64 * h + 8 * s:64 * h + 8 * s + 8] = e
    put("inv", inv[:, None])
    b = np.zeros((P, C2W), np.float32)

    def put2(name, v):
        o, w = C2[name]
        b[:, o:o + w] = v

    t = np.arange(T, dtype=np.float32)
    f = np.float32(10000.0) ** (-np.arange(128, dtype=np.float32) / np.float32(128))
    ang = (f[:, None] * t[None, :]).astype(np.float32)
    put2("cosA", np.cos(ang.astype(np.float64)))
    put2("sinA", np.sin(ang.astype(np.float64)))
    f = np.float32(10000.0) ** (-np.arange(32, dtype=np.float32) / np.float32(32))
    ang = np.tile((f[:, None] * t[None, :]).astype(np.float32), (4, 1))
    put2("cosB", np.cos(ang.astype(np.float64)))
    put2("sinB", np.sin(ang.astype(np.float64)))
    dec = []
    for h in range(4):
        lg = np.log1p(-2.0 ** (-5.0 - h))
        d = np.arange(T)[None, :] - r[:, None]
        m = np.where(d >= 0, np.exp(np.maximum(d, 0) * lg), 0.0) / 16.0
        dec += [m, m[:, 0:128]]
    put2("dec", np.concatenate(dec, 1))
    return a, b


def lay_weights(i):
    def tile(w, nf):
        k, f = w.shape
        kt, nch = k // P, f // (nf * P)
        return np.ascontiguousarray(w.reshape(kt, P, nch, nf * P).transpose(2, 1, 0, 3)).reshape(nch, P, kt * nf * P)

    def cols(w, *idx):
        return np.concatenate([w[:, a:b] for a, b in idx], 1)

    win = i["w_in"][0]
    z0 = 1536
    W = {}
    W["ada"] = tile(i["w_ada"][0], 4)
    W["in_wag"] = tile(win[:, z0 + 1536:z0 + 1792], 2)
    W["in_rkv"] = tile(win[:, z0:z0 + 1536], 4)
    W["in_v"] = tile(win[:, 1024:1536], 4)
    W["in_qk"] = tile(win[:, 0:1024], 4)
    W["in_g"] = tile(win[:, 3328:5376], 4)
    W["pm"] = tile(i["w_proj_moba"][0], 8)
    W["pr"] = tile(i["w_proj_rwkv"][0], 8)
    W["wo"] = tile(i["w_out"][0], 4)
    W["wq"] = tile(i["peer_wq"][0], 4)
    W["sub"] = np.ascontiguousarray(i["peer_subkeys"][0].transpose(3, 0, 1, 2)).reshape(1, P, 2048)
    W["u"] = tile(i["peer_u"][0].T, 4)
    W["v"] = np.ascontiguousarray(i["peer_v"][0].reshape(32, 4, P, 1024).transpose(0, 2, 1, 3)).reshape(32, P, 4096)
    a = i["a_w_in_2"][0]
    W["a_qk"] = tile(a[:, 0:2048], 4)
    W["a_v"] = tile(a[:, 2048:4096], 4)
    W["a_g"] = tile(a[:, 4096:6144], 4)
    W["a_o"] = tile(i["a_w_out_2"][0], 2)
    d = i["kv_w_down_2"]
    W["kvd"] = tile(d[:, 0:512], 4)
    W["kvr"] = tile(cols(d, (512, 576), (512, 576)), 1)
    up = i["kv_w_up_2"].reshape(512, 16, 256)
    W["kvk"] = tile(up[:, :, 0:128].reshape(512, 2048), 8)
    W["kvv"] = tile(up[:, :, 128:256].reshape(512, 2048), 8)
    b = i["b_w_in_2"][0]
    W["b_q4"] = tile(b[:, 0:512], 4)
    W["b_q2"] = tile(b[:, 512:768], 2)
    W["b_g"] = tile(b[:, 768:2816], 4)
    uq = i["b_w_uq_2"][0].reshape(768, 16, 192)
    W["uqn"] = tile(uq[:, :, 0:128].reshape(768, 2048), 4)
    W["uqr"] = tile(uq[:, :, 128:192].reshape(768, 1024), 4)
    W["b_o"] = tile(i["b_w_out_2"][0], 2)
    for n, w in W.items():
        kt, nf, nch = WEIGHTS[n]
        assert w.shape == (nch, P, kt * nf * P), (n, w.shape)
    return W


def lay_vectors(i):
    def v(x, n):
        return np.asarray(x).reshape(n, P).T

    mu = i["rwkv_mu"][0]
    mus = np.concatenate([mu[1536:1792], mu[0:1536]])
    parts = {
        "c": v(i["c"][0], 8), "b_ada": v(i["b_ada"][0], 48), "n1": v(i["norm1_g"][0], 8), "n2": v(i["norm2_g"][0], 8),
        "qg": np.tile(i["q_norm_g"][0], 2)[:, None], "kg": np.tile(i["k_norm_g"][0], 2)[:, None],
        "mu": v(mus, 14), "w0": v(i["rwkv_w0"][0], 4), "a0": v(i["rwkv_a0"][0], 4), "k_k": v(i["rwkv_k_k"][0], 4),
        "k_a": v(i["rwkv_k_a"][0], 4), "r_k": v(i["rwkv_r_k"][0].reshape(512), 4), "ln_g": v(i["rwkv_ln_g"][0], 4),
        "ln_b": v(i["rwkv_ln_b"][0], 4), "bq": v(i["b_q_norm_2"][0], 6), "kvn": v(i["kv_norm_2"], 4),
        "g2": v(i["ln_g_2"].reshape(2048), 16), "b2": v(i["ln_b_2"].reshape(2048), 16),
    }
    return np.ascontiguousarray(np.concatenate([parts[n] for n in VEC], 1))


def lay_inputs(inputs):
    i = {k: np.asarray(v) for k, v in inputs.items()}
    m = lay_weights(i)
    m["xT"] = np.ascontiguousarray(i["x"][0].T.reshape(8, P, T).transpose(1, 0, 2)).reshape(P, 8 * T)
    m["vec"] = lay_vectors(i)
    m["con"], m["con2"] = constants()
    m["w2a2"] = np.concatenate([i["rwkv_w2"][0], i["rwkv_a2"][0]], 0)
    m["g2"] = i["rwkv_g2"][0]
    m["pos"] = np.ascontiguousarray(np.broadcast_to(i["positions"], (P, T)))
    return {k: np.ascontiguousarray(v) for k, v in m.items()}


def kernel(**inputs):
    import concourse.bacc as _bacc
    from concourse.bass_utils import run_bass_kernel_spmd as _run

    nc = _bacc.Bacc("TRN2", target_bir_lowering=False, num_devices=1)
    arrays = {f"in_{k}": v for k, v in lay_inputs(inputs).items()}
    D = {k[3:]: nc.dram_tensor(k, list(v.shape), mybir.dt.from_np(v.dtype), kind="ExternalInput").ap()
         for k, v in arrays.items()}
    out = nc.dram_tensor("out_0", [P, 8 * T], F32, kind="ExternalOutput").ap()
    build_program(nc, D, out)
    r = _run(nc, [arrays], core_ids=[0])
    y = np.asarray(r.results[0]["out_0"])
    return np.ascontiguousarray(y.reshape(P, 8, T).transpose(2, 1, 0)).reshape(1, T, 1024)
```
